# Optimizing a Trainium2 kernel written in Bass

```python
import jax, jax.numpy as jnp
from jax import lax
import numpy as np

D_MODEL = 1024
BATCH = 1
SEQ = 1024
DEPTH = 1

N_MIXERS = 2
N_HGRN = (DEPTH + N_MIXERS - 1) // N_MIXERS
N_CONV = DEPTH // N_MIXERS
HGRN_EXPAND = 128
HGRN_HEADS = D_MODEL // HGRN_EXPAND
HGRN_DK = HGRN_EXPAND
HGRN_FDIM = HGRN_HEADS * HGRN_DK
HGRN_DV = D_MODEL // HGRN_HEADS
HGRN_CHUNK = 64
CONV_WIDTH = 31
FFN_CONV_WIDTH = 3
D_FF = 2816
N_MOD = 6
EPS = 1e-6

kernel_name = "hybrid_hgrn2_conformer_convffn_adaln"

def rmsnorm(x, g):
    xf = x.astype(jnp.float32)
    y = xf * lax.rsqrt(jnp.mean(xf * xf, axis=-1, keepdims=True) + EPS)
    return (y * g).astype(x.dtype)

def layernorm(x, g, b):
    xf = x.astype(jnp.float32)
    mu = jnp.mean(xf, axis=-1, keepdims=True)
    var = jnp.mean(jnp.square(xf - mu), axis=-1, keepdims=True)
    y = (xf - mu) * lax.rsqrt(var + EPS)
    return (y * g + b).astype(x.dtype)

def causal_dwconv(x, w, b):
    width, ch = w.shape
    y = lax.conv_general_dilated(
        x, w[:, None, :].astype(x.dtype), window_strides=(1,), padding=[(width - 1, 0)],
        dimension_numbers=("NWC", "WIO", "NWC"), feature_group_count=ch)
    return y + b

def hgrn2_mixer(h, w_in, lb, gnorm_g, w_out):
    B, T, _ = h.shape
    nc = T // HGRN_CHUNK
    proj = h @ w_in
    q, fz, i, g = jnp.split(proj, [HGRN_FDIM, 2 * HGRN_FDIM, 2 * HGRN_FDIM + D_MODEL], axis=-1)
    q = jax.nn.silu(q.astype(jnp.float32))
    f = lb + (1.0 - lb) * jax.nn.sigmoid(fz.astype(jnp.float32))
    k = 1.0 - f
    logf = jnp.log(f)
    v = i.astype(jnp.float32)

    def to_chunks(a, d):
        a = a.reshape(B, nc, HGRN_CHUNK, HGRN_HEADS, d)
        return jnp.transpose(a, (1, 0, 3, 2, 4))

    qc, kc, gc = to_chunks(q, HGRN_DK), to_chunks(k, HGRN_DK), to_chunks(logf, HGRN_DK)
    vc = to_chunks(v, HGRN_DV)
    causal = jnp.tril(jnp.ones((HGRN_CHUNK, HGRN_CHUNK), dtype=bool))[:, :, None]

    def step(S, inp):
        qb, kb, vb, gb = inp
        bcum = jnp.cumsum(gb, axis=2)
        diff = bcum[:, :, :, None, :] - bcum[:, :, None, :, :]
        decay = jnp.exp(jnp.where(causal, diff, -jnp.inf))
        scores = jnp.einsum("bhtd,bhtsd,bhsd->bhts", qb, decay, kb)
        o = jnp.einsum("bhts,bhsv->bhtv", scores, vb)
        o = o + jnp.einsum("bhtd,bhdv->bhtv", qb * jnp.exp(bcum), S)
        bend = bcum[:, :, -1]
        S_new = jnp.exp(bend)[..., None] * S + jnp.einsum(
            "bhsd,bhsv->bhdv", kb * jnp.exp(bend[:, :, None, :] - bcum), vb)
        return S_new, o

    S0 = jnp.zeros((B, HGRN_HEADS, HGRN_DK, HGRN_DV), jnp.float32)
    _, oc = lax.scan(step, S0, (qc, kc, vc, gc))
    o = jnp.transpose(oc, (1, 0, 3, 2, 4)).reshape(B, T, HGRN_HEADS, HGRN_DV)
    o = rmsnorm(o, gnorm_g).reshape(B, T, D_MODEL)
    o = o * jax.nn.silu(g.astype(jnp.float32))
    return o.astype(h.dtype) @ w_out

def conformer_conv_mixer(h, w_in, b_in, dw_w, dw_b, ln_g, ln_b, w_out, b_out):
    u = h @ w_in + b_in
    a, gt = jnp.split(u, 2, axis=-1)
    u = a * jax.nn.sigmoid(gt)
    u = causal_dwconv(u, dw_w, dw_b)
    u = jax.nn.silu(layernorm(u, ln_g, ln_b))
    return u @ w_out + b_out

def conv_ffn(h, w_up, dw_w, dw_b, w_down):
    u = causal_dwconv(h @ w_up, dw_w, dw_b)
    a, b = jnp.split(u, 2, axis=-1)
    return (jax.nn.silu(a) * b) @ w_down

def setup_inputs(seed: int = 0) -> dict:
    key = jax.random.key(seed)
    ks = jax.random.split(key, 24)
    D, F = D_MODEL, D_FF
    nrm = lambda k, shape, s: jax.random.normal(k, shape, jnp.float32) * s
    return {
        "x": nrm(ks[0], (BATCH, SEQ, D), 1.0),
        "c": nrm(ks[1], (BATCH, D), 1.0),
        "ada_w": nrm(ks[2], (DEPTH, D, N_MOD * D), 0.5 * D ** -0.5),
        "ada_b": nrm(ks[3], (DEPTH, N_MOD * D), 0.02),
        "pre_mix_g": 1.0 + nrm(ks[4], (DEPTH, D), 0.02),
        "post_mix_g": 1.0 + nrm(ks[5], (DEPTH, D), 0.02),
        "pre_ffn_g": 1.0 + nrm(ks[6], (DEPTH, D), 0.02),
        "post_ffn_g": 1.0 + nrm(ks[7], (DEPTH, D), 0.02),
        "hgrn_w_in": nrm(ks[8], (N_HGRN, D, 2 * HGRN_FDIM + 2 * D), D ** -0.5),
        "hgrn_lb_logits": nrm(ks[9], (DEPTH + 1, HGRN_FDIM), 1.0),
        "hgrn_gnorm_g": 1.0 + nrm(ks[10], (N_HGRN, HGRN_DV), 0.02),
        "hgrn_w_out": nrm(ks[11], (N_HGRN, D, D), D ** -0.5),
        "conv_w_in": nrm(ks[12], (N_CONV, D, 2 * D), D ** -0.5),
        "conv_b_in": nrm(ks[13], (N_CONV, 2 * D), 0.02),
        "conv_dw_w": nrm(ks[14], (N_CONV, CONV_WIDTH, D), CONV_WIDTH ** -0.5),
        "conv_dw_b": nrm(ks[15], (N_CONV, D), 0.02),
        "conv_ln_g": 1.0 + nrm(ks[16], (N_CONV, D), 0.02),
        "conv_ln_b": nrm(ks[17], (N_CONV, D), 0.02),
        "conv_w_out": nrm(ks[18], (N_CONV, D, D), D ** -0.5),
        "conv_b_out": nrm(ks[19], (N_CONV, D), 0.02),
        "ffn_w_up": nrm(ks[20], (DEPTH, D, 2 * F), D ** -0.5),
        "ffn_dw_w": nrm(ks[21], (DEPTH, FFN_CONV_WIDTH, 2 * F), FFN_CONV_WIDTH ** -0.5),
        "ffn_dw_b": nrm(ks[22], (DEPTH, 2 * F), 0.02),
        "ffn_w_down": nrm(ks[23], (DEPTH, F, D), F ** -0.5),
    }

def reference(x, c, ada_w, ada_b, pre_mix_g, post_mix_g, pre_ffn_g, post_ffn_g,
              hgrn_w_in, hgrn_lb_logits, hgrn_gnorm_g, hgrn_w_out,
              conv_w_in, conv_b_in, conv_dw_w, conv_dw_b, conv_ln_g, conv_ln_b,
              conv_w_out, conv_b_out, ffn_w_up, ffn_dw_w, ffn_dw_b, ffn_w_down):
    lb_all = jnp.cumsum(jax.nn.softmax(hgrn_lb_logits.astype(jnp.float32), axis=0), axis=0)
    cond = jax.nn.silu(c)
    for i in range(DEPTH):
        mod = (cond @ ada_w[i] + ada_b[i])[:, None, :]
        sh1, sc1, g1, sh2, sc2, g2 = jnp.split(mod, N_MOD, axis=-1)
        h = rmsnorm(x, pre_mix_g[i]) * (1.0 + sc1) + sh1
        j = i // N_MIXERS
        if i % N_MIXERS == 0:
            y = hgrn2_mixer(h, hgrn_w_in[j], lb_all[i], hgrn_gnorm_g[j], hgrn_w_out[j])
        else:
            y = conformer_conv_mixer(h, conv_w_in[j], conv_b_in[j], conv_dw_w[j], conv_dw_b[j],
                                     conv_ln_g[j], conv_ln_b[j], conv_w_out[j], conv_b_out[j])
        x = x + g1 * rmsnorm(y, post_mix_g[i])
        h = rmsnorm(x, pre_ffn_g[i]) * (1.0 + sc2) + sh2
        y = conv_ffn(h, ffn_w_up[i], ffn_dw_w[i], ffn_dw_b[i], ffn_w_down[i])
        x = x + g2 * rmsnorm(y, post_ffn_g[i])
    return x


_drawn_inputs = setup_inputs


def setup_inputs(seed=0):
    import zlib

    import numpy as np

    out = dict(_drawn_inputs(seed))
    spreads = {}
    factors = {'pre_mix_g': 7.453,
     'post_mix_g': 8.0,
     'pre_ffn_g': 20.739,
     'post_ffn_g': 34.09,
     'hgrn_gnorm_g': 8.0,
     'ffn_dw_b': 21.505}
    for name, (base, spread) in spreads.items():
        noise = np.random.default_rng([zlib.crc32(name.encode()), seed]).standard_normal(out[name].shape)
        drawn = base * np.exp(spread * noise) if base else spread * noise
        out[name] = __import__('jax').numpy.asarray(drawn.astype(out[name].dtype))
    for name, factor in factors.items():
        out[name] = (out[name] * factor).astype(out[name].dtype)
    return out
```

```python
from contextlib import ExitStack

import concourse.bass as bass
from concourse import mybir

ALU = mybir.AluOpType
ACT = mybir.ActivationFunctionType
F32 = mybir.dt.float32
F32R = mybir.dt.float32r
I32 = mybir.dt.int32
AX_X = mybir.AxisListType.X

P = 128
EPS = 1e-6
BANK = 512


class Tally:

    def __init__(self):
        self.base, self.n = 0, 0

    def up(self):
        self.n += 1
        return 1

    @property
    def now(self):
        return self.base + self.n

    def restart(self, base):
        self.base, self.n = base, 0


def hybrid_layer(nc, x, c, ada_w, ada_b, pre_mix_g, post_mix_g, pre_ffn_g, post_ffn_g,
                 w_in, lb_logits, gnorm_g, w_out, w_up, dw_w, dw_b, w_down, out):
    T, D = x.shape[1], x.shape[2]
    NT = T // P
    KD = D // P
    H = KD
    F = w_down.shape[1]
    FT = F // P
    TH = T // BANK
    LEVELS = 7
    AC = BANK
    JH = KD // 2
    START_PIECES = 2 * D // AC
    PIECES = 6 * D // AC
    assert T == 1024 and D == 1024 and FT * P == F and NT == 8 and TH == 2 and PIECES - START_PIECES == H

    x_rows = x.rearrange("b (n p) d -> (b n) p d", p=P)
    out_rows = out.rearrange("b (n p) d -> (b n) p d", p=P)
    ada_cols = ada_w.rearrange("l (j p) n -> p (l j) n", p=P)
    w_in_cols = w_in.rearrange("l (k p) n -> p (l k) n", p=P)
    w_out_rows = w_out.rearrange("l (k p) n -> (l k) p n", p=P)
    w_up_cols = w_up.rearrange("l (k p) n -> p (l k) n", p=P)
    w_down_rows = w_down.rearrange("l (k p) n -> (l k) p n", p=P)
    Q_COL, F_COL, I_COL, G_COL = 0, D, 2 * D, 3 * D
    x1_rows = nc.dram_tensor("x_after_mixer", (NT, P, D), F32, kind="Internal").ap()

    ctx = ExitStack()
    with ctx:
        def sb(name, shape, dt=F32, where=None):
            return (where or ctx).enter_context(nc.sbuf_tensor(name, shape, dt))

        def sem(name):
            return ctx.enter_context(nc.semaphore(name))

        ident = sb("ident", [P, P])
        ones = sb("ones", [P, P])
        level_mask = sb("level_mask", [P, LEVELS, P // 2])
        minus_half = sb("minus_half", [P, 8])
        VR = 5 * KD + 1
        vec_cols = sb("vec_cols", [P, VR])
        dw_cols = sb("dw_cols", [P, 4, 2 * FT])
        mix_scale = sb("mix_scale", [P, KD])
        mix_shift = sb("mix_shift", [P, KD])
        ffn_scale = sb("ffn_scale", [P, KD])
        ffn_shift = sb("ffn_shift", [P, KD])
        low = sb("low", [P, H])
        high = sb("high", [P, H])
        cond = sb("cond", [P, KD])
        tiny = sb("tiny", [P, 8, 8])
        stat = sb("stat", [P, 8, 8])
        mod_rows = sb("mod_rows", [P, 4, D])
        mod_flat = mod_rows[:, :, :].rearrange("p v d -> p (v d)")

        early = ExitStack()
        hT = sb("hT", [P, 2, KD, T], F32R, early)

        mixer = ExitStack()
        oT = sb("oT", [P, H, T], F32, mixer)
        head = ExitStack()
        w_split = sb("w_split", [P, 2, 2, KD, P], F32R, head)
        w_raw = sb("w_raw", [P, 2, KD, P], F32, head)
        ada_raw = sb("ada_raw", [P, 2, JH, AC], F32, head)
        f_dec = sb("f_dec", [P, T], F32, head)
        q_act = sb("q_act", [P, T], F32, head)
        gate = sb("gate", [P, T], F32, head)
        ada_acc = sb("ada_acc", [P, AC], F32, head)
        ada_bias = sb("ada_bias", [1, AC], F32, head)
        k_dec = sb("k_dec", [P, T], F32, head)
        q_dec = sb("q_dec", [P, T], F32, head)
        v_tok = sb("v_tok", [P, NT, P], F32, head)
        tok = sb("tok", [P, NT, P], F32, head)
        scores = sb("scores", [P, T], F32, head)
        g_act = sb("g_act", [P, T], F32, head)
        totals = sb("totals", [P, T], F32, head)
        states = sb("states", [P, NT - 1, P], F32, head)
        x_sb = oT
        vec_rows = tok[0:VR, 0, :]
        dw_rows = g_act[0:2 * FT, 0:4 * P].rearrange("n (t p) -> n t p", t=4)
        h_f32 = [q_dec, k_dec]
        head.close()

        project = ExitStack()
        slabs = sb("slabs", [P, 3, D], F32, project)
        wo_split = sb("wo_split", [P, KD, 2, D], F32R, project)
        o_split = sb("o_split", [P, 2, 2, KD // 2, P], F32R, project)
        norm_tile = slabs[:, 0, :]
        project.close()
        mixer.close()

        up = ExitStack()
        up_split = sb("up_split", [P, 2, 2, KD, P], F32R, up)
        up_raw = sb("up_raw", [P, 2, KD, P], F32, up)
        act = sb("act", [P, FT, T], F32, up)
        conv_a, conv_b, sig_a = mod_rows[:, 0, :], mod_rows[:, 1, :], mod_rows[:, 2, :]
        up.close()
        early.close()

        down = ExitStack()
        a_split = sb("a_split", [P, 2, 2, T], F32R, down)
        wd_split = sb("wd_split", [P, 2, 2, BANK], F32R, down)
        wd_raw = sb("wd_raw", [P, 2, BANK], F32, down)
        y_left = sb("y_left", [P, NT, BANK], F32, down)
        x1_in = sb("x1_in", [P, 2, D], F32, down)
        out_sb = sb("out_sb", [P, 2, D], F32, down)
        down.close()

        ps = ctx.enter_context(nc.psum_tensor("ps", [P, 8, BANK], F32))

        def pair(n):
            return ps[:, 2 * n:2 * n + 2, :].rearrange("p a b -> p (a b)")

        vec_in = sem("vec_in")
        dw_in = sem("dw_in")
        x_in = [sem(f"x_in{i}") for i in range(NT)]
        w_in_arrived = [sem(f"w_in_arrived{s}") for s in range(2)]
        ada_in = [sem(f"ada_in{s}") for s in range(2)]
        post_in = sem("post_in")
        wo_in = [sem(f"wo_in{s}") for s in range(3)]
        xt_in = [sem(f"xt_in{u}") for u in range(2)]
        x1_stored = [sem(f"x1_stored{u}") for u in range(2)]
        up_in = [sem(f"up_in{s}") for s in range(2)]
        wd_in = [sem(f"wd_in{s}") for s in range(2)]
        x1_back = [sem(f"x1_back{u}") for u in range(2)]
        out_stored = [sem(f"out_stored{u}") for u in range(2)]

        pool_own = sem("pool_own")
        consts_made = sem("consts_made")
        rooted = sem("rooted")

        dve_own = sem("dve_own")
        act_own = sem("act_own")
        vecs_turned = sem("vecs_turned")
        dw_turned = sem("dw_turned")
        vecs_copied = sem("vecs_copied")
        lb_shifted = sem("lb_shifted")
        lb_exp = sem("lb_exp")
        c_sig = sem("c_sig")
        x_squared = sem("x_squared")
        x_mean = sem("x_mean")
        x_normed = sem("x_normed")
        x_turned = sem("x_turned")
        h_scaled = sem("h_scaled")
        h_split = sem("h_split")
        ada_used = sem("ada_used")
        ada_summed = sem("ada_summed")
        ada_spread = sem("ada_spread")
        ada_rowed = sem("ada_rowed")
        mod_turned = sem("mod_turned")
        mods_made = sem("mods_made")

        w_hi = sem("w_hi")
        w_lo = sem("w_lo")
        projected = sem("projected")
        sig_done = sem("sig_done")
        sig_used = sem("sig_used")
        values_copied = sem("values_copied")
        values_turned = sem("values_turned")
        v_ready = sem("v_ready")
        decayed = sem("decayed")
        scored = sem("scored")
        masked = sem("masked")
        keys_turned = sem("keys_turned")
        keys_ready = sem("keys_ready")
        chunk_kv = sem("chunk_kv")
        states_ready = sem("states_ready")
        o_ready = sem("o_ready")
        o_squared = sem("o_squared")
        o_mean = sem("o_mean")
        o_normed = sem("o_normed")
        o_turned = sem("o_turned")
        head_out = sem("head_out")

        wo_hi = sem("wo_hi")
        wo_lo = sem("wo_lo")
        o_hi = [sem(f"o_hi{q}") for q in range(2)]
        o_lo = [sem(f"o_lo{q}") for q in range(2)]
        o_used = [sem(f"o_used{q}") for q in range(2)]
        y_squared = sem("y_squared")
        y_mean = sem("y_mean")
        x1_made = sem("x1_made")
        x1_squared = sem("x1_squared")
        x1_mean = sem("x1_mean")
        x1_normed = sem("x1_normed")
        x1_turned = sem("x1_turned")
        h2_scaled = sem("h2_scaled")
        h2_split = sem("h2_split")

        up_hi = [sem(f"up_hi{s}") for s in range(2)]
        up_lo = [sem(f"up_lo{s}") for s in range(2)]
        upped = [sem(f"upped{s}") for s in range(2)]
        tap0 = [sem(f"tap0{s}") for s in range(2)]
        conved = [sem(f"conved{s}") for s in range(2)]
        a_sig = sem("a_sig")
        gated = sem("gated")

        a_hi = sem("a_hi")
        a_lo = sem("a_lo")
        wd_hi = sem("wd_hi")
        wd_lo = sem("wd_lo")
        downed = sem("downed")
        y_bank = sem("y_bank")
        out_squared = sem("out_squared")
        left_kept = sem("left_kept")
        out_mean = sem("out_mean")
        out_rooted = sem("out_rooted")
        out_made = sem("out_made")

        block = ctx.enter_context(nc.Block())

        @block.sync
        def _(sp):
            for i, rows in enumerate((c, pre_mix_g, pre_ffn_g)):
                sp.dma_start(vec_rows[i * KD:(i + 1) * KD, :],
                             rows.rearrange("a (k p) -> (a k) p", p=P)).then_inc(vec_in, 16)
            sp.dma_start(vec_rows[3 * KD:5 * KD, :],
                         lb_logits.rearrange("a (k p) -> (a k) p", p=P)).then_inc(vec_in, 16)
            sp.dma_start(vec_rows[5 * KD:VR, :], gnorm_g).then_inc(vec_in, 16)
            sp.dma_start(dw_rows[:, 0:3, :], dw_w.rearrange("a t (n p) -> n (a t) p", p=P)).then_inc(dw_in, 16)
            sp.dma_start(dw_rows[:, 3, :], dw_b.rearrange("a (n p) -> (a n) p", p=P)).then_inc(dw_in, 16)

            def load_w(n, col):
                sp.dma_start(w_raw[:, n % 2, :, :], w_in_cols[:, :, col]).then_inc(w_in_arrived[n % 2], 16)

            def load_piece(p, k):
                for s in range(2):
                    if not isinstance(k, int) or k > 0:
                        sp.wait_ge(ada_used, 2 * k - 1 + s)
                    sp.dma_start(ada_raw[:, s, :, :],
                                 ada_cols[:, s * JH:(s + 1) * JH, bass.ts(p, AC)]).then_inc(ada_in[s], 16)
                    if s == 1:
                        if not isinstance(k, int) or k > 0:
                            sp.wait_ge(ada_summed, k)
                        sp.dma_start(ada_bias[:, :], ada_b[:, bass.ts(p, AC)]).then_inc(ada_in[1], 16)

            for i in range(NT):
                sp.dma_start(x_sb[:, i, :], x_rows[i]).then_inc(x_in[i], 16)
            load_w(0, slice(F_COL, F_COL + P))
            load_w(1, slice(Q_COL, Q_COL + P))
            for p in range(START_PIECES):
                load_piece(p, p)
            sp.wait_ge(w_lo, 1)
            load_w(2, slice(I_COL, I_COL + P))
            sp.wait_ge(w_lo, 2)
            load_w(3, slice(G_COL, G_COL + P))
            load_piece(START_PIECES, START_PIECES)
            with sp.Fori(0, H - 1) as h:
                sp.wait_ge(w_lo, 4 * h + 3)
                load_w(0, bass.ds(F_COL + P + h * P, P))
                sp.wait_ge(w_lo, 4 * h + 4)
                load_w(1, bass.ds(Q_COL + P + h * P, P))
                load_piece(h + START_PIECES + 1, h + START_PIECES + 1)
                sp.wait_ge(w_lo, 4 * h + 5)
                load_w(0, bass.ds(I_COL + P + h * P, P))
                sp.wait_ge(w_lo, 4 * h + 6)
                load_w(1, bass.ds(G_COL + P + h * P, P))

            sp.wait_ge(projected, 4 * H)
            sp.dma_start(slabs[:, 0, :], post_mix_g.broadcast_to((P, D))).then_inc(post_in, 16)
            sp.dma_start(slabs[:, 1, :], post_ffn_g.broadcast_to((P, D))).then_inc(post_in, 16)
            for k in range(KD):
                s = (k + 2) % 3
                if k in (1, 2):
                    sp.wait_ge(mods_made, 2 + k)
                if k >= 3:
                    sp.wait_ge(wo_lo, k - 2)
                sp.dma_start(slabs[:, s, :], w_out_rows[k]).then_inc(wo_in[s], 16)
            sp.wait_ge(wo_lo, KD)
            sp.dma_start(slabs[:, 1, :], x_rows[0]).then_inc(xt_in[0], 16)
            sp.dma_start(slabs[:, 2, :], x_rows[1]).then_inc(xt_in[1], 16)
            with sp.Fori(0, NT // 2 - 1) as ii:
                for u in range(2):
                    sp.wait_ge(x1_made, 2 * ii + u + 1)
                    sp.dma_start(x1_rows[2 * ii + u], mod_rows[:, 1 + u, :]).then_inc(x1_stored[u], 16)
                    sp.dma_start(slabs[:, 1 + u, :], x_rows[2 * ii + u + 2]).then_inc(xt_in[u], 16)
            sp.wait_ge(o_lo[1], NT)
            sp.dma_start(up_raw[:, 0, :, :], w_up_cols[:, :, 0:P]).then_inc(up_in[0], 16)
            sp.dma_start(up_raw[:, 1, :, :], w_up_cols[:, :, F:F + P]).then_inc(up_in[1], 16)
            for u in range(2):
                sp.wait_ge(x1_made, NT - 1 + u)
                sp.dma_start(x1_rows[NT - 2 + u], mod_rows[:, 1 + u, :]).then_inc(x1_stored[u], 16)
            with sp.Fori(0, FT - 1) as j:
                for s in range(2):
                    sp.wait_ge(up_lo[s], j + 1)
                    sp.dma_start(up_raw[:, s, :, :],
                                 w_up_cols[:, :, bass.ds(s * F + P + j * P, P)]).then_inc(up_in[s], 16)

            sp.wait_ge(upped[1], FT)
            for s in range(2):
                sp.dma_start(wd_raw[:, s, :], w_down_rows[s, :, 0:BANK]).then_inc(wd_in[s], 16)
            for u in range(2):
                sp.wait_ge(x1_stored[u], 16 * NT // 2)
                sp.dma_start(x1_in[:, u, :], x1_rows[u]).then_inc(x1_back[u], 16)
            with sp.Fori(0, FT // 2 - 1) as kk:
                for s in range(2):
                    sp.wait_ge(wd_lo, 2 * kk + s + 1)
                    sp.dma_start(wd_raw[:, s, :], w_down_rows[2 * kk + s + 2, :, 0:BANK]).then_inc(wd_in[s], 16)
            for s in range(2):
                sp.wait_ge(wd_lo, FT - 1 + s)
                sp.dma_start(wd_raw[:, s, :], w_down_rows[s, :, BANK:D]).then_inc(wd_in[s], 16)
            with sp.Fori(0, FT // 2 - 1) as kk:
                for s in range(2):
                    sp.wait_ge(wd_lo, FT + 2 * kk + s + 1)
                    sp.dma_start(wd_raw[:, s, :], w_down_rows[2 * kk + s + 2, :, BANK:D]).then_inc(wd_in[s], 16)
            for t in range(NT):
                sp.wait_ge(out_made, t + 1)
                sp.dma_start(out_rows[t], out_sb[:, t % 2, :]).then_inc(out_stored[t % 2], 16)
                if t + 2 < NT:
                    sp.dma_start(x1_in[:, t % 2, :], x1_rows[t + 2]).then_inc(x1_back[t % 2], 16)
            for u in range(2):
                sp.wait_ge(out_stored[u], 16 * NT // 2)

        @block.gpsimd
        def _(pool):
            own = Tally()
            pool.memset(ident[:, :], 0.0).then_inc(pool_own, own.up())
            pool.memset(level_mask[:, :, :], 1.0).then_inc(pool_own, own.up())
            pool.memset(ones[:, :], 1.0).then_inc(consts_made, 1)
            pool.memset(minus_half[:, :], -0.5).then_inc(consts_made, 1)
            pool.wait_ge(pool_own, own.now)
            pool.affine_select(out=ident[:, :], in_=ident[:, :], compare_op=ALU.not_equal, fill=1.0, base=0,
                               pattern=[[-1, P]], channel_multiplier=1).then_inc(consts_made, 1)
            for j in range(LEVELS):
                half = 1 << j
                m = level_mask[:, j, :].rearrange("p (n w) -> p n w", w=half)
                blocks = P // (2 * half)
                pool.affine_select(out=m, in_=m, compare_op=ALU.is_ge, fill=0.0, base=0,
                                   pattern=[[-2 * half, blocks], [0, half]],
                                   channel_multiplier=1).then_inc(pool_own, own.up())
                pool.wait_ge(pool_own, own.now)
                pool.affine_select(out=m, in_=m, compare_op=ALU.is_ge, fill=0.0, base=half - 1,
                                   pattern=[[2 * half, blocks], [0, half]],
                                   channel_multiplier=-1).then_inc(consts_made, 1)
            pool.memset(scores[:, :], 0.0).then_inc(consts_made, 1)
            pool.wait_ge(consts_made, 2)
            pool.wait_ge(x_mean, 1)
            pool.tensor_tensor(stat[:, 0, :], tiny[:, 0, :], minus_half[:, :], ALU.pow).then_inc(rooted, 1)
            with pool.Fori(0, H) as h:
                pool.wait_ge(o_mean, h + 1)
                pool.tensor_tensor(stat[:, 1, :], tiny[:, 1, :], minus_half[:, :], ALU.pow).then_inc(rooted, 1)
            with pool.Fori(0, NT) as i:
                pool.wait_ge(y_mean, i + 1)
                pool.tensor_tensor(stat[:, 2, 0:1], tiny[:, 2, 0:1], minus_half[:, 0:1],
                                   ALU.pow).then_inc(rooted, 1)
                pool.wait_ge(x1_mean, i + 1)
                pool.tensor_tensor(stat[:, 3, 0:1], tiny[:, 3, 0:1], minus_half[:, 0:1],
                                   ALU.pow).then_inc(rooted, 1)
            for t in range(NT):
                pool.wait_ge(out_mean, t + 1)
                pool.tensor_tensor(stat[:, 4, t:t + 1], tiny[:, 4, t:t + 1], minus_half[:, 0:1],
                                   ALU.pow).then_inc(out_rooted, 1)

        @block.scalar
        def _(sa):
            for i in range(NT):
                sa.wait_ge(x_in[i], 16)
                if i > 0:
                    sa.wait_ge(x_squared, i)
                sa.activation(q_dec[:, :], x_sb[:, i, :], ACT.Square,
                              accum_out=tiny[:, 5, i:i + 1]).then_inc(x_squared, 1)
            sa.wait_ge(lb_shifted, 1)
            sa.activation(stat[:, 5:7, :], stat[:, 5:7, :], ACT.Exp).then_inc(lb_exp, 1)
            sa.activation(cond[:, :], vec_cols[:, 0:KD], ACT.Sigmoid).then_inc(c_sig, 1)

            def split_w(n, s, load):
                sa.wait_ge(w_in_arrived[s], 16 * load)
                if not isinstance(n, int) or n >= 2:
                    sa.wait_ge(projected, n - 1)
                sa.activation(w_split[:, s, 0, :, :], w_raw[:, s, :, :], ACT.Copy).then_inc(w_hi, 1)

            def ada_row(p, dst):
                sa.wait_ge(ada_spread, p + 1)
                sa.activation(mod_flat[:, bass.ts(dst, AC)], ps[:, 6, :], ACT.Copy).then_inc(ada_rowed, 1)

            split_w(0, 0, 1)
            split_w(1, 1, 1)
            for p in range(START_PIECES):
                ada_row(p, p)
            sa.wait_ge(mods_made, 1)
            for k in range(KD):
                sa.wait_ge(x_turned, k + 1)
                if k >= 2:
                    sa.wait_ge(h_split, k - 1)
                sa.activation(h_f32[k % 2][:, :], pair(k % 2), ACT.Identity, bias=mix_shift[:, k:k + 1],
                              scale=mix_scale[:, k:k + 1]).then_inc(h_scaled, 1)

            def sigmoid_f(h):
                sa.wait_ge(projected, 4 * h + 1)
                if not isinstance(h, int) or h > 0:
                    sa.wait_ge(sig_used, 3 * h)
                sa.activation(gate[:, :], pair(0), ACT.Sigmoid).then_inc(sig_done, 1)

            def head_front(h):
                sa.wait_ge(projected, 4 * h + 2)
                sa.wait_ge(sig_used, 3 * h + 1)
                sa.activation(gate[:, :], pair(1), ACT.Sigmoid).then_inc(sig_done, 1)
                split_w(4 * h + 3, 1, 2 * h + 2)
                sa.wait_ge(projected, 4 * h + 3)
                sa.wait_ge(sig_used, 3 * h + 2)
                sa.activation(gate[:, :], pair(0), ACT.Copy).then_inc(values_copied, 1)

            def head_values(h):
                sa.wait_ge(values_turned, h + 1)
                sa.activation(v_tok[:, :, :].rearrange("p n d -> p (n d)"), pair(3), ACT.Copy).then_inc(v_ready, 1)

            def sigmoid_g(h):
                sa.wait_ge(projected, 4 * h + 4)
                sa.activation(gate[:, :], pair(1), ACT.Sigmoid).then_inc(sig_done, 1)

            def head_keys(h):
                sa.wait_ge(keys_turned, h + 1)
                sa.activation(tok[:, :, :].rearrange("p n d -> p (n d)"), pair(3), ACT.Copy).then_inc(keys_ready, 1)

            def head_square(h):
                sa.wait_ge(o_ready, h + 1)
                sa.activation(tok[:, :, :].rearrange("p n d -> p (n d)"), pair(3), ACT.Square).then_inc(o_squared, 1)

            sigmoid_f(0)
            split_w(2, 0, 2)
            with sa.Fori(0, H - 1) as h:
                head_front(h)
                split_w(4 * h + 4, 0, 2 * h + 3)
                head_values(h)
                sigmoid_g(h)
                split_w(4 * h + 5, 1, 2 * h + 3)
                head_keys(h)
                ada_row(START_PIECES + h, h)
                sigmoid_f(h + 1)
                head_square(h)
                split_w(4 * h + 6, 0, 2 * h + 4)
            head_front(H - 1)
            head_values(H - 1)
            sigmoid_g(H - 1)
            head_keys(H - 1)
            ada_row(PIECES - 1, H - 1)
            head_square(H - 1)

            for k in range(KD):
                s = (k + 2) % 3
                sa.wait_ge(wo_in[s], 16 * (k // 3 + 1))
                if k == 0:
                    sa.wait_ge(sig_used, 3 * H)
                    sa.wait_ge(ada_rowed, PIECES)
                if k == 4:
                    sa.wait_ge(head_out, H)
                sa.activation(wo_split[:, k, 0, :], slabs[:, s, :], ACT.Copy).then_inc(wo_hi, 1)

            def split_o(i, q):
                if not isinstance(i, int) or i > 0:
                    sa.wait_ge(o_used[q], i)
                sa.activation(o_split[:, q, 0, :, :],
                              oT[:, q * (KD // 2):(q + 1) * (KD // 2), bass.ts(i, P)],
                              ACT.Copy).then_inc(o_hi[q], 1)

            def square_y(i, u):
                sa.wait_ge(o_used[1], i + 1)
                sa.activation(pair(3), pair(u), ACT.Square, accum_out=tiny[:, 6, 0:1]).then_inc(y_squared, 1)

            def scale_h2(i):
                sa.wait_ge(x1_turned, i + 1)
                for k in range(KD):
                    done = sa.activation(norm_tile[:, k * P:(k + 1) * P], pair(2)[:, k * P:(k + 1) * P],
                                         ACT.Identity, bias=ffn_shift[:, k:k + 1], scale=ffn_scale[:, k:k + 1])
                done.then_inc(h2_scaled, 1)

            def norm_x1(i, u):
                sa.wait_ge(x1_made, i + 1)
                sa.activation(pair(3), mod_rows[:, 1 + u, :], ACT.Square,
                              accum_out=tiny[:, 7, 0:1]).then_inc(x1_squared, 1)
                if not isinstance(i, int) or i > 0:
                    sa.wait_ge(h2_split, i)
                sa.wait_ge(rooted, 1 + H + 2 * i + 2)
                sa.activation(norm_tile, mod_rows[:, 1 + u, :], ACT.Copy,
                              scale=stat[:, 3, 0:1]).then_inc(x1_normed, 1)

            split_o(0, 0)
            split_o(0, 1)
            sa.wait_ge(mods_made, 5)
            split_o(1, 0)
            square_y(0, 0)
            split_o(1, 1)
            norm_x1(0, 0)

            def mixer_tile(i, u):
                split_o(i + 1, 0)
                square_y(i, u)
                split_o(i + 1, 1)
                scale_h2(i - 1)
                norm_x1(i, u)

            mixer_tile(1, 1)
            with sa.Fori(1, NT // 2 - 1) as ii:
                for u in range(2):
                    mixer_tile(2 * ii + u, u)
            mixer_tile(NT - 2, 0)

            def split_up(j, s):
                sa.wait_ge(up_in[s], 16 * (j + 1))
                if not isinstance(j, int) or j > 0:
                    sa.wait_ge(upped[s], j)
                sa.activation(up_split[:, s, 0, :, :], up_raw[:, s, :, :], ACT.Copy).then_inc(up_hi[s], 1)

            sa.wait_ge(o_lo[1], NT)
            split_up(0, 0)
            split_up(0, 1)
            square_y(NT - 1, 1)
            scale_h2(NT - 2)
            norm_x1(NT - 1, 1)
            scale_h2(NT - 1)

            def first_tap(j, s, dst):
                ft = j + s * FT
                sa.wait_ge(upped[s], j + 1)
                if not isinstance(j, int) or j > 0:
                    sa.wait_ge(gated, j)
                sa.activation(dst, pair(s), ACT.Identity, bias=dw_cols[:, 3, bass.ds(ft, 1)],
                              scale=dw_cols[:, 2, bass.ds(ft, 1)]).then_inc(tap0[s], 1)

            def sigmoid_a(j):
                sa.wait_ge(conved[0], j + 1)
                sa.activation(sig_a, conv_a, ACT.Sigmoid).then_inc(a_sig, 1)

            for u in range(2):
                sa.wait_ge(x1_stored[u], 16 * NT // 2)
            first_tap(0, 0, conv_a)
            split_up(1, 0)
            sigmoid_a(0)
            first_tap(0, 1, conv_b)
            split_up(1, 1)
            with sa.Fori(1, FT - 1) as j:
                first_tap(j, 0, conv_a)
                split_up(j + 1, 0)
                sigmoid_a(j)
                first_tap(j, 1, conv_b)
                split_up(j + 1, 1)
            first_tap(FT - 1, 0, conv_a)
            sigmoid_a(FT - 1)

            def split_down(kk, k, s, load):
                if not isinstance(kk, int) or kk >= 2:
                    sa.wait_ge(downed, kk - 1)
                sa.activation(a_split[:, s, 0, :], act[:, k, :], ACT.Copy).then_inc(a_hi, 1)
                sa.wait_ge(wd_in[s], 16 * load)
                sa.activation(wd_split[:, s, 0, :], wd_raw[:, s, :], ACT.Copy).then_inc(wd_hi, 1)

            def square_out(half, t):
                sa.wait_ge(y_bank, half * NT + t + 1)
                sa.activation(y_left[:, t, :] if half == 0 else out_sb[:, t % 2, 0:BANK], ps[:, t, :], ACT.Square,
                              accum_out=tiny[:, half, t:t + 1]).then_inc(out_squared, 1)

            sa.wait_ge(upped[1], FT)
            sa.wait_ge(gated, 2)
            split_down(0, 0, 0, 1)
            split_down(1, 1, 1, 1)
            first_tap(FT - 1, 1, conv_b)
            with sa.Fori(1, FT // 2 - 1) as kk:
                for s in range(2):
                    split_down(2 * kk + s, 2 * kk + s, s, kk + 1)
            sa.wait_ge(gated, FT)
            split_down(FT - 2, FT - 2, 0, FT // 2)
            split_down(FT - 1, FT - 1, 1, FT // 2)
            split_down(FT, 0, 0, FT // 2 + 1)
            for t in range(NT):
                square_out(0, t)
            split_down(FT + 1, 1, 1, FT // 2 + 1)
            with sa.Fori(1, FT // 2) as kk:
                for s in range(2):
                    split_down(FT + 2 * kk + s, 2 * kk + s, s, kk + (FT // 2 + 1))
            for t in range(NT):
                if t >= 2:
                    sa.wait_ge(out_stored[t % 2], 16 * (t // 2))
                square_out(1, t)

        @block.vector
        def _(ve):
            own = Tally()

            def link(ins):
                ins.then_inc(dve_own, own.up())
                ve.wait_ge(dve_own, own.now)

            ve.wait_ge(vecs_turned, 1)
            ve.tensor_copy(vec_cols[:, :], ps[:, 4, 0:VR]).then_inc(vecs_copied, 1)
            ve.wait_ge(vecs_copied, 1)
            l0, l1 = vec_cols[:, 3 * KD:4 * KD], vec_cols[:, 4 * KD:5 * KD]
            e0, e1 = stat[:, 5, :], stat[:, 6, :]
            link(ve.tensor_tensor(stat[:, 7, :], l0, l1, ALU.max))
            ve.tensor_tensor(e0, l0, stat[:, 7, :], ALU.subtract)
            ve.tensor_tensor(e1, l1, stat[:, 7, :], ALU.subtract).then_inc(lb_shifted, 1)
            ve.wait_ge(dw_turned, 1)
            ve.tensor_copy(dw_cols[:, :, :].rearrange("p t n -> p (t n)"), ps[:, 5, 0:8 * FT]).then_inc(vecs_copied, 1)
            ve.wait_ge(lb_exp, 1)
            link(ve.tensor_tensor(stat[:, 7, :], e0, e1, ALU.add))
            link(ve.reciprocal(stat[:, 7, :], stat[:, 7, :]))
            link(ve.tensor_tensor(low[:, :], e0, stat[:, 7, :], ALU.mult))
            ve.tensor_scalar(high[:, :], low[:, :], -1.0, 1.0, ALU.mult, ALU.add)
            ve.wait_ge(c_sig, 1)
            link(ve.tensor_tensor(cond[:, :], cond[:, :], vec_cols[:, 0:KD], ALU.mult))

            ve.wait_ge(x_squared, NT)
            ve.tensor_scalar(tiny[:, 0, :], tiny[:, 5, :], 1.0 / D, EPS, ALU.mult, ALU.add).then_inc(x_mean, 1)
            ve.wait_ge(rooted, 1)
            for i in range(NT):
                ve.tensor_scalar(x_sb[:, i, :], x_sb[:, i, :], stat[:, 0, i:i + 1], None,
                                 ALU.mult).then_inc(x_normed, 1)

            def split_w(n, s):
                ve.wait_ge(w_hi, n + 1)
                ve.tensor_tensor(w_split[:, s, 1, :, :], w_raw[:, s, :, :], w_split[:, s, 0, :, :].bitcast(F32),
                                 ALU.subtract).then_inc(w_lo, 1)

            def ada_piece(p):
                acc = ada_acc[:, :]
                for s in range(2):
                    ve.wait_ge(ada_in[s], 16 * (s + 1) * (p + 1))
                    for j in range(JH):
                        k = s * JH + j
                        if k == 0:
                            if not isinstance(p, int) or p > 0:
                                ve.wait_ge(ada_spread, p)
                            ins = ve.tensor_scalar(acc, ada_raw[:, s, j, :], cond[:, k:k + 1], None, ALU.mult)
                        else:
                            ins = ve.scalar_tensor_tensor(out=acc, in0=ada_raw[:, s, j, :], scalar=cond[:, k:k + 1],
                                                          in1=acc, op0=ALU.mult, op1=ALU.add)
                        if j == JH - 1:
                            ins.then_inc(ada_used, 1)
                            ve.wait_ge(ada_used, 2 * p + s + 1)
                        else:
                            link(ins)
                ve.tensor_tensor(ada_acc[0:1, :], ada_acc[0:1, :], ada_bias[:, :], ALU.add).then_inc(ada_summed, 1)

            split_w(0, 0)
            split_w(1, 1)
            for p in range(START_PIECES):
                if p > 0:
                    ve.wait_ge(ada_summed, p)
                ada_piece(p)

            def modulation(shift, scale, gain):
                ve.tensor_copy(shift[:, :], ps[:, 5, 0:KD])
                return ve.scalar_tensor_tensor(out=scale[:, :], in0=ps[:, 5, KD:2 * KD], scalar=1.0, in1=gain,
                                               op0=ALU.add, op1=ALU.mult)

            ve.wait_ge(mod_turned, 1)
            modulation(mix_shift, mix_scale, vec_cols[:, KD:2 * KD]).then_inc(mods_made, 1)
            for k in range(KD):
                ve.wait_ge(h_scaled, k + 1)
                link(ve.tensor_copy(hT[:, 0, k, :], h_f32[k % 2][:, :]))
                ve.tensor_tensor(hT[:, 1, k, :], h_f32[k % 2][:, :], hT[:, 0, k, :].bitcast(F32),
                                 ALU.subtract).then_inc(h_split, 1)

            def forget(h):
                ve.wait_ge(sig_done, 3 * h + 1)
                ve.tensor_scalar(f_dec[:, :], gate[:, :], high[:, bass.ds(h, 1)], low[:, bass.ds(h, 1)],
                                 ALU.mult, ALU.add).then_inc(sig_used, 1)

            def mask(n, bank_n):
                if n == 0:
                    ve.copy_predicated(scores[:, :].rearrange("p (c t) -> p c t", t=P),
                                       ident[:, :].bitcast(I32).unsqueeze(1).broadcast_to((P, NT, P)),
                                       pair(2).rearrange("p (c t) -> p c t", t=P)).then_inc(masked, 1)
                    return
                half = 1 << (n - 1)
                ve.copy_predicated(
                    scores[:, :].rearrange("p (n two w) -> p n two w", two=2, w=half)[:, :, 1, :],
                    level_mask[:, n - 1, :].bitcast(I32).unsqueeze(1).broadcast_to((P, NT, P // 2)),
                    ps[:, bank_n, :].rearrange("p (n w) -> p n w", w=half)).then_inc(masked, 1)

            TOTAL_AT = [None, 0] + [T - (T >> (j - 1)) for j in range(2, LEVELS + 1)]

            def total(j):
                n = T >> j
                return f_dec[:, :] if j == 0 else totals[:, TOTAL_AT[j]:TOTAL_AT[j] + n]

            def take_level(h, n):
                j = n - 1
                half = 1 << j
                tj = total(j).rearrange("p (n two) -> p n two", two=2)
                blocks = T // (2 * half)
                right = q_dec[:, :].rearrange("p (n two w) -> p n two w", two=2, w=half)[:, :, 1, :]
                left = k_dec[:, :].rearrange("p (n two w) -> p n two w", two=2, w=half)[:, :, 0, :]
                ve.wait_ge(decayed, 8 * h + n)
                ve.wait_ge(scored, 8 * h + n + 1)
                if n > 1:
                    ve.wait_ge(masked, 8 * h + n)
                ve.tensor_tensor(total(j + 1).unsqueeze(2), tj[:, :, 0:1], tj[:, :, 1:2], ALU.mult)
                if n == 1:
                    mask(0, None)
                    ve.wait_ge(masked, 8 * h + 1)
                ve.tensor_tensor(right, right, tj[:, :, 0:1].broadcast_to((P, blocks, half)), ALU.mult)
                ve.tensor_tensor(left, left, tj[:, :, 1:2].broadcast_to((P, blocks, half)),
                                 ALU.mult).then_inc(decayed, 1)
                mask(n, level_bank[n])

            level_bank = [None, 6, 7, 4, 5, 4, 5, 4]

            def head_start(h):
                ve.wait_ge(sig_used, 3 * h + 1)
                ve.tensor_scalar(k_dec[:, :], f_dec[:, :], -1.0, 1.0, ALU.mult, ALU.add)
                ve.wait_ge(sig_done, 3 * h + 2)
                ve.tensor_tensor(q_act[:, :], pair(1), gate[:, :], ALU.mult).then_inc(sig_used, 1)
                ve.wait_ge(sig_used, 3 * h + 2)
                ve.tensor_tensor(q_dec[:, :], q_act[:, :], f_dec[:, :], ALU.mult).then_inc(decayed, 1)
                split_w(4 * h + 3, 1)
                for n in (1, 2):
                    take_level(h, n)

            def gate_out(h):
                ve.wait_ge(sig_done, 3 * h + 3)
                ve.tensor_tensor(g_act[:, :], pair(1), gate[:, :], ALU.mult).then_inc(sig_used, 1)

            def head_states(h):
                tot = total(LEVELS)
                kv = pair(2).rearrange("p (c d) -> p c d", d=P)
                ve.wait_ge(chunk_kv, h + 1)
                link(ve.tensor_copy(states[:, 0, :], kv[:, 0, :]))
                for ch in range(1, NT - 1):
                    ins = ve.scalar_tensor_tensor(out=states[:, ch, :], in0=states[:, ch - 1, :],
                                                  scalar=tot[:, ch:ch + 1], in1=kv[:, ch, :],
                                                  op0=ALU.mult, op1=ALU.add)
                    if ch < NT - 2:
                        link(ins)
                ins.then_inc(states_ready, 1)

            def head_norm(h):
                o = pair(3).rearrange("p (c d) -> p c d", d=P)
                ve.wait_ge(o_squared, h + 1)
                link(ve.reduce_sum(tiny[:, 2, :], tok[:, :, :], axis=AX_X))
                ve.tensor_scalar(tiny[:, 1, :], tiny[:, 2, :], 1.0 / P, EPS, ALU.mult, ALU.add).then_inc(o_mean, 1)
                ve.wait_ge(rooted, h + 2)
                ve.tensor_tensor(tok[:, :, :], o, stat[:, 1, :].unsqueeze(2).broadcast_to((P, NT, P)),
                                 ALU.mult).then_inc(o_normed, 1)

            def head_end(h):
                ve.wait_ge(o_turned, h + 1)
                ve.wait_ge(sig_used, 3 * h + 3)
                ve.scalar_tensor_tensor(out=oT[:, h, :], in0=pair(2), scalar=vec_cols[:, 5 * KD:VR],
                                        in1=g_act[:, :], op0=ALU.mult, op1=ALU.mult).then_inc(head_out, 1)

            forget(0)
            split_w(2, 0)
            ve.wait_ge(ada_summed, START_PIECES)
            ada_piece(START_PIECES)
            base, per = own.now, (NT - 2) + 1 + 2 * (JH - 1)
            with ve.Fori(0, H - 1) as h:
                own.restart(base + h * per)
                head_start(h)
                split_w(4 * h + 4, 0)
                for n in range(3, LEVELS + 1):
                    take_level(h, n)
                gate_out(h)
                split_w(4 * h + 5, 1)
                head_states(h)
                forget(h + 1)
                head_norm(h)
                split_w(4 * h + 6, 0)
                head_end(h)
                ve.wait_ge(ada_summed, START_PIECES + h + 1)
                ada_piece(START_PIECES + h + 1)
                assert own.n == per
            own.restart(base + (H - 1) * per)
            last = H - 1
            head_start(last)
            for n in range(3, LEVELS + 1):
                take_level(last, n)
            gate_out(last)
            head_states(last)
            head_norm(last)
            head_end(last)

            ve.wait_ge(mod_turned, 2)
            modulation(ffn_shift, ffn_scale, vec_cols[:, 2 * KD:3 * KD]).then_inc(mods_made, 1)
            ve.wait_ge(post_in, 32)
            ve.wait_ge(ada_rowed, PIECES)
            ve.tensor_tensor(mod_rows[:, 0, :], mod_rows[:, 0, :], slabs[:, 0, :], ALU.mult).then_inc(mods_made, 1)
            ve.tensor_tensor(mod_rows[:, 3, :], mod_rows[:, 3, :], slabs[:, 1, :], ALU.mult).then_inc(mods_made, 1)
            for k in range(KD):
                s = (k + 2) % 3
                ve.wait_ge(wo_hi, k + 1)
                ve.tensor_tensor(wo_split[:, k, 1, :], slabs[:, s, :], wo_split[:, k, 0, :].bitcast(F32),
                                 ALU.subtract).then_inc(wo_lo, 1)
            ve.wait_ge(mods_made, 4)
            ve.memset(tiny[:, 3, 0:1], 1.0).then_inc(mods_made, 1)

            def split_o(i, q):
                ve.wait_ge(o_hi[q], i + 1)
                ve.tensor_tensor(o_split[:, q, 1, :, :],
                                 oT[:, q * (KD // 2):(q + 1) * (KD // 2), bass.ts(i, P)],
                                 o_split[:, q, 0, :, :].bitcast(F32), ALU.subtract).then_inc(o_lo[q], 1)

            def make_x1(i, u, times):
                x1 = mod_rows[:, 1 + u, :]
                ve.wait_ge(y_squared, i + 1)
                ve.tensor_scalar(tiny[:, 2, 0:1], tiny[:, 6, 0:1], 1.0 / D, EPS,
                                 ALU.mult, ALU.add).then_inc(y_mean, 1)
                if not isinstance(times, int) or times > 0:
                    ve.wait_ge(x1_stored[u], 16 * times)
                ve.wait_ge(rooted, 1 + H + 2 * i + 1)
                link(ve.scalar_tensor_tensor(out=x1, in0=pair(u), scalar=stat[:, 2, 0:1], in1=mod_rows[:, 0, :],
                                             op0=ALU.mult, op1=ALU.mult))
                ve.wait_ge(xt_in[u], 16 * (times + 1))
                ve.tensor_tensor(x1, x1, slabs[:, 1 + u, :], ALU.add).then_inc(x1_made, 1)

            def mean_x1(i):
                ve.wait_ge(x1_squared, i + 1)
                ve.tensor_scalar(tiny[:, 3, 0:1], tiny[:, 7, 0:1], 1.0 / D, EPS,
                                 ALU.mult, ALU.add).then_inc(x1_mean, 1)

            def split_h2(i):
                h2 = norm_tile.rearrange("p (k t) -> p k t", t=P)
                hi, lo = hT[:, 0, :, bass.ts(i, P)], hT[:, 1, :, bass.ts(i, P)]
                ve.wait_ge(h2_scaled, i + 1)
                link(ve.tensor_copy(hi, h2))
                ve.tensor_tensor(lo, h2, hi.bitcast(F32), ALU.subtract).then_inc(h2_split, 1)

            split_o(0, 0)
            split_o(0, 1)
            split_o(1, 0)
            make_x1(0, 0, 0)
            split_o(1, 1)
            mean_x1(0)

            def mixer_tile(i, u, times):
                split_o(i + 1, 0)
                make_x1(i, u, times)
                split_o(i + 1, 1)
                split_h2(i - 1)
                mean_x1(i)

            mixer_tile(1, 1, 0)
            base, per = own.now, 4
            with ve.Fori(1, NT // 2 - 1) as ii:
                own.restart(base + (ii - 1) * per)
                for u in range(2):
                    mixer_tile(2 * ii + u, u, ii)
                assert own.n == per
            own.restart(base + (NT // 2 - 2) * per)
            mixer_tile(NT - 2, 0, NT // 2 - 1)

            def split_up(j, s):
                ve.wait_ge(up_hi[s], j + 1)
                ve.tensor_tensor(up_split[:, s, 1, :, :], up_raw[:, s, :, :],
                                 up_split[:, s, 0, :, :].bitcast(F32), ALU.subtract).then_inc(up_lo[s], 1)

            split_up(0, 0)
            split_up(0, 1)
            make_x1(NT - 1, 1, NT // 2 - 1)
            split_h2(NT - 2)
            mean_x1(NT - 1)
            split_h2(NT - 1)

            def more_taps(j, s, dst):
                ft = j + s * FT
                ve.wait_ge(tap0[s], j + 1)
                link(ve.scalar_tensor_tensor(out=dst[:, 1:T], in0=pair(s)[:, 0:T - 1],
                                             scalar=dw_cols[:, 1, bass.ds(ft, 1)], in1=dst[:, 1:T],
                                             op0=ALU.mult, op1=ALU.add))
                ve.scalar_tensor_tensor(out=dst[:, 2:T], in0=pair(s)[:, 0:T - 2],
                                        scalar=dw_cols[:, 0, bass.ds(ft, 1)], in1=dst[:, 2:T],
                                        op0=ALU.mult, op1=ALU.add).then_inc(conved[s], 1)

            def gate_ffn(j):
                ve.wait_ge(conved[1], j + 1)
                link(ve.tensor_tensor(conv_b, conv_b, conv_a, ALU.mult))
                ve.wait_ge(a_sig, j + 1)
                ve.tensor_tensor(act[:, j, :], conv_b, sig_a, ALU.mult).then_inc(gated, 1)

            base, per = own.now, 3
            with ve.Fori(0, FT - 1) as j:
                own.restart(base + j * per)
                more_taps(j, 0, conv_a)
                split_up(j + 1, 0)
                more_taps(j, 1, conv_b)
                split_up(j + 1, 1)
                gate_ffn(j)
                assert own.n == per
            own.restart(base + (FT - 1) * per)
            more_taps(FT - 1, 0, conv_a)

            def split_down(kk, k, s):
                ve.wait_ge(a_hi, kk + 1)
                ve.tensor_tensor(a_split[:, s, 1, :], act[:, k, :], a_split[:, s, 0, :].bitcast(F32),
                                 ALU.subtract).then_inc(a_lo, 1)
                ve.wait_ge(wd_hi, kk + 1)
                ve.tensor_tensor(wd_split[:, s, 1, :], wd_raw[:, s, :], wd_split[:, s, 0, :].bitcast(F32),
                                 ALU.subtract).then_inc(wd_lo, 1)

            split_down(0, 0, 0)
            split_down(1, 1, 1)
            more_taps(FT - 1, 1, conv_b)
            gate_ffn(FT - 1)
            with ve.Fori(1, FT // 2) as kk:
                for s in range(2):
                    split_down(2 * kk + s, 2 * kk + s, s)
            split_down(FT, 0, 0)
            g2 = mod_rows[:, 3, :]
            for t in range(NT):
                ve.wait_ge(out_squared, t + 1)
                ve.tensor_tensor(y_left[:, t, :], ps[:, t, :], g2[:, 0:BANK], ALU.mult).then_inc(left_kept, 1)
            split_down(FT + 1, 1, 1)
            with ve.Fori(1, FT // 2) as kk:
                for s in range(2):
                    split_down(FT + 2 * kk + s, 2 * kk + s, s)

            def finish(t):
                o, x1 = out_sb[:, t % 2, :], x1_in[:, t % 2, :]
                ve.wait_ge(out_rooted, t + 1)
                ve.wait_ge(x1_back[t % 2], 16 * (t // 2 + 1))
                ve.scalar_tensor_tensor(out=o[:, 0:BANK], in0=y_left[:, t, :], scalar=stat[:, 4, t:t + 1],
                                        in1=x1[:, 0:BANK], op0=ALU.mult, op1=ALU.add)
                ve.scalar_tensor_tensor(out=o[:, BANK:D], in0=o[:, BANK:D], scalar=stat[:, 4, t:t + 1],
                                        in1=x1[:, BANK:D], op0=ALU.mult, op1=ALU.add).then_inc(out_made, 1)

            for t in range(NT):
                ve.wait_ge(out_squared, NT + t + 1)
                link(ve.tensor_tensor(tiny[:, 5, t:t + 1], tiny[:, 0, t:t + 1], tiny[:, 1, t:t + 1], ALU.add))
                ve.tensor_scalar(tiny[:, 4, t:t + 1], tiny[:, 5, t:t + 1], 1.0 / D, EPS,
                                 ALU.mult, ALU.add).then_inc(out_mean, 1)
                link(ve.tensor_tensor(out_sb[:, t % 2, BANK:D], ps[:, t, :], g2[:, BANK:D], ALU.mult))
                finish(t)

        @block.tensor
        def _(pe):
            HI, LO = 0, 1
            PARTS = ((HI, HI), (HI, LO), (LO, HI))

            def turn(dst, src, n=P):
                return pe.transpose(dst, src, ident[0:n, 0:n])

            pe.wait_ge(consts_made, 3 + LEVELS + 1)
            pe.wait_ge(vec_in, 16 * 5)
            turn(ps[:, 4, 0:VR], vec_rows, VR).then_inc(vecs_turned, 1)
            pe.wait_ge(dw_in, 32)
            for t in range(4):
                last = turn(ps[:, 5, 2 * FT * t:2 * FT * (t + 1)], dw_rows[:, t, :], 2 * FT)
            last.then_inc(dw_turned, 1)

            def spread(p):
                pe.wait_ge(ada_summed, p + 1)
                if not isinstance(p, int) or p > 0:
                    pe.wait_ge(ada_rowed, p)
                pe.matmul(ps[:, 6, :], ones[:, :], ada_acc[:, :], start=True, stop=True).then_inc(ada_spread, 1)

            def turn_mods(row):
                for v in range(2):
                    for k in range(KD):
                        last = turn(ps[:, 5, v * KD + k:v * KD + k + 1],
                                    mod_rows[0:1, row + v, k * P:(k + 1) * P], 1)
                last.then_inc(mod_turned, 1)

            for p in range(START_PIECES):
                spread(p)
            pe.wait_ge(ada_rowed, START_PIECES)
            pe.wait_ge(vecs_copied, 2)
            turn_mods(0)
            pe.wait_ge(x_normed, NT)
            for k in range(KD):
                if k >= 2:
                    pe.wait_ge(h_scaled, k - 1)
                for i in range(NT):
                    last = turn(pair(k % 2)[:, i * P:(i + 1) * P], x_sb[:, i, k * P:(k + 1) * P])
                last.then_inc(x_turned, 1)

            def project_quarter(s, half, kh, done=None):
                for k in range(kh * (KD // 2), (kh + 1) * (KD // 2)):
                    for n, (a, b) in enumerate(PARTS):
                        last = pe.matmul(ps[:, 2 * s + half, :], w_split[:, s, a, k, :],
                                         hT[:, b, k, half * BANK:(half + 1) * BANK],
                                         start=(k == 0 and n == 0), stop=(k == KD - 1 and n == 2))
                if done is not None:
                    last.then_inc(done, 1)

            def group(s, quarter, n, freed=None, count=None):
                if quarter == 0:
                    pe.wait_ge(w_lo, n + 1)
                    if freed is not None:
                        pe.wait_ge(freed, count)
                project_quarter(s, quarter // 2, quarter % 2, projected if quarter == 3 else None)

            def chunk(ap, ch):
                return ap[:, ch * P:(ch + 1) * P]

            def diagonal(h):
                pe.wait_ge(decayed, 8 * h + 1)
                for ch in range(NT):
                    last = pe.matmul(chunk(pair(2), ch), chunk(k_dec, ch), chunk(q_act, ch), start=True, stop=True)
                last.then_inc(scored, 1)

            def level(h, n, bank_n, masked_n=None):
                half = 1 << (n - 1)
                pe.wait_ge(decayed, 8 * h + n)
                if masked_n is not None:
                    pe.wait_ge(masked, 8 * h + masked_n)
                for ch in range(NT):
                    moving = chunk(q_dec, ch).rearrange("p (n two w) -> p n two w", two=2, w=half)[:, :, 1, :]
                    last = pe.matmul(ps[:, bank_n, ch * (P // 2):(ch + 1) * (P // 2)], chunk(k_dec, ch), moving,
                                     start=True, stop=True)
                last.then_inc(scored, 1)

            def turn_values(h):
                pe.wait_ge(values_copied, h + 1)
                pe.wait_ge(masked, 8 * h + 3)
                for ch in range(NT):
                    last = turn(chunk(pair(3), ch), chunk(gate, ch))
                last.then_inc(values_turned, 1)

            def turn_keys(h):
                pe.wait_ge(decayed, 8 * h + 8)
                pe.wait_ge(v_ready, h + 1)
                for ch in range(NT):
                    last = turn(chunk(pair(3), ch), chunk(k_dec, ch))
                last.then_inc(keys_turned, 1)

            def keys_values(h):
                pe.wait_ge(keys_ready, h + 1)
                pe.wait_ge(masked, 8 * h + 8)
                for ch in range(NT - 1):
                    last = pe.matmul(chunk(pair(2), ch), tok[:, ch, :], v_tok[:, ch, :], start=True, stop=True)
                last.then_inc(chunk_kv, 1)

            def outputs(h):
                pe.wait_ge(ada_rowed, START_PIECES + h + 1)
                pe.wait_ge(states_ready, h + 1)
                for ch in range(NT):
                    last = pe.matmul(chunk(pair(3), ch), chunk(scores, ch), v_tok[:, ch, :],
                                     start=True, stop=(ch == 0))
                    if ch > 0:
                        last = pe.matmul(chunk(pair(3), ch), chunk(q_dec, ch), states[:, ch - 1, :],
                                         start=False, stop=True)
                last.then_inc(o_ready, 1)

            def turn_outputs(h):
                pe.wait_ge(o_normed, h + 1)
                for ch in range(NT):
                    last = turn(chunk(pair(2), ch), tok[:, ch, :])
                last.then_inc(o_turned, 1)

            pe.wait_ge(w_lo, 1)
            for quarter in range(4):
                if quarter < 2:
                    pe.wait_ge(h_split, KD // 2 * (quarter + 1))
                if quarter == 0:
                    pe.wait_ge(h_scaled, KD)
                group(0, quarter, 0)
            for quarter in range(4):
                group(1, quarter, 1)

            def head_first_half(h):
                for quarter in range(4):
                    group(0, quarter, 4 * h + 2, sig_done, 3 * h + 1)
                    if quarter == 1:
                        diagonal(h)
                        level(h, 1, 6)
                    if quarter == 2:
                        level(h, 2, 7)
                    if quarter == 3:
                        level(h, 3, 4, 1)
                for quarter in range(4):
                    group(1, quarter, 4 * h + 3, sig_used, 3 * h + 2)
                    if quarter == 0:
                        turn_values(h)
                        level(h, 4, 5)
                    if quarter == 1:
                        level(h, 5, 4, 4)
                    if quarter == 2:
                        level(h, 6, 5, 5)
                    if quarter == 3:
                        level(h, 7, 4, 6)

            with pe.Fori(0, H - 1) as h:
                head_first_half(h)
                for quarter in range(4):
                    group(0, quarter, 4 * h + 4, values_copied, h + 1)
                    if quarter == 0:
                        turn_keys(h)
                    if quarter == 1:
                        keys_values(h)
                    if quarter == 2:
                        spread(START_PIECES + h)
                    if quarter == 3:
                        outputs(h)
                for quarter in range(4):
                    group(1, quarter, 4 * h + 5, sig_used, 3 * h + 3)
                    if quarter == 1:
                        turn_outputs(h)
            last_head = H - 1
            head_first_half(last_head)
            turn_keys(last_head)
            keys_values(last_head)
            spread(PIECES - 1)
            outputs(last_head)
            turn_outputs(last_head)
            pe.wait_ge(ada_rowed, PIECES)
            pe.wait_ge(head_out, H)
            turn_mods(1)

            def mix_out(i, u, first=False):
                if first:
                    pe.wait_ge(mods_made, 2)
                for q in range(2):
                    pe.wait_ge(o_lo[q], i + 1)
                    for kq in range(KD // 2):
                        k = q * (KD // 2) + kq
                        if first:
                            pe.wait_ge(wo_lo, k + 1)
                        for half in range(2):
                            for n, (a, b) in enumerate(PARTS):
                                last = pe.matmul(ps[:, 2 * u + half, :], o_split[:, q, a, kq, :],
                                                 wo_split[:, k, b, half * BANK:(half + 1) * BANK],
                                                 start=(k == 0 and n == 0), stop=(k == KD - 1 and n == 2))
                    last.then_inc(o_used[q], 1)

            def turn_x1(i):
                pe.wait_ge(x1_normed, i + 1)
                for k in range(KD):
                    last = turn(chunk(pair(2), k), chunk(norm_tile, k))
                last.then_inc(x1_turned, 1)

            mix_out(0, 0, True)
            mix_out(1, 1)
            turn_x1(0)
            with pe.Fori(0, NT // 2 - 1) as ii:
                for u in range(2):
                    i = 2 * ii + 2 + u
                    pe.wait_ge(x1_made, 2 * ii + u + 1)
                    mix_out(i, u)
                    turn_x1(i - 1)

            def up_half(s, half, done=None):
                for k in range(KD):
                    for n, (a, b) in enumerate(PARTS):
                        last = pe.matmul(ps[:, 2 * s + half, :], up_split[:, s, a, k, :],
                                         hT[:, b, k, half * BANK:(half + 1) * BANK],
                                         start=(k == 0 and n == 0), stop=(k == KD - 1 and n == 2))
                if done is not None:
                    last.then_inc(done, 1)

            pe.wait_ge(x1_made, NT - 1)
            pe.wait_ge(up_lo[0], 1)
            pe.wait_ge(h2_split, NT // 2)
            up_half(0, 0)
            pe.wait_ge(x1_made, NT)
            pe.wait_ge(up_lo[1], 1)
            up_half(1, 0)
            turn_x1(NT - 1)
            pe.wait_ge(h2_split, NT)
            up_half(0, 1, upped[0])
            up_half(1, 1, upped[1])
            with pe.Fori(1, FT) as j:
                for s in range(2):
                    pe.wait_ge(up_lo[s], j + 1)
                    pe.wait_ge(conved[s], j)
                    up_half(s, 0)
                    up_half(s, 1, upped[s])

            def down_step(kk, s, start=False, stop=False, half=0):
                pe.wait_ge(a_lo, kk + 1)
                pe.wait_ge(wd_lo, kk + 1)
                for t in range(NT):
                    if start and half == 1:
                        pe.wait_ge(left_kept, t + 1)
                    if start and half == 0 and t in (0, 2):
                        pe.wait_ge(conved[t // 2], FT)
                    for n, (a, b) in enumerate(PARTS):
                        last = pe.matmul(ps[:, t, :], a_split[:, s, a, t * P:(t + 1) * P], wd_split[:, s, b, :],
                                         start=(start and n == 0), stop=(stop and n == 2))
                    if stop:
                        last.then_inc(y_bank, 1)
                if not stop:
                    last.then_inc(downed, 1)

            def down_half(half):
                base = half * FT
                down_step(base, 0, start=True, half=half)
                down_step(base + 1, 1)
                with pe.Fori(1, FT // 2 - 1) as kk:
                    for s in range(2):
                        down_step(base + 2 * kk + s, s)
                down_step(base + FT - 2, 0)
                down_step(base + FT - 1, 1, stop=True)

            down_half(0)
            down_half(1)


_INS = ["x", "c", "ada_w", "ada_b", "pre_mix_g", "post_mix_g", "pre_ffn_g", "post_ffn_g", "hgrn_w_in",
        "hgrn_lb_logits", "hgrn_gnorm_g", "hgrn_w_out", "ffn_w_up", "ffn_dw_w", "ffn_dw_b", "ffn_w_down"]


def kernel(**inputs):
    import numpy as _np
    import concourse.bacc as _bacc
    from concourse import mybir as _mybir
    from concourse.bass_utils import run_bass_kernel_spmd as _run

    nc = _bacc.Bacc("TRN2", target_bir_lowering=False, num_devices=1)
    arrays, args = {}, []
    for name in _INS:
        a = _np.ascontiguousarray(inputs[name])
        arrays[f"in_{name}"] = a
        args.append(nc.dram_tensor(f"in_{name}", a.shape, _mybir.dt.from_np(a.dtype), kind="ExternalInput").ap())
    shape = arrays["in_x"].shape
    args.append(nc.dram_tensor("out_x", shape, _mybir.dt.from_np(_np.dtype("float32")), kind="ExternalOutput").ap())
    hybrid_layer(nc, *args)
    r = _run(nc, [arrays], core_ids=[0])
    return r.results[0]["out_x"]
```

```python
from contextlib import ExitStack

import concourse.bass as bass
from concourse import mybir

ALU = mybir.AluOpType
ACT = mybir.ActivationFunctionType
F32 = mybir.dt.float32
F32R = mybir.dt.float32r
I32 = mybir.dt.int32
AX_X = mybir.AxisListType.X

P = 128
EPS = 1e-6
BANK = 512


class Tally:

    def __init__(self):
        self.base, self.n = 0, 0

    def up(self):
        self.n += 1
        return 1

    @property
    def now(self):
        return self.base + self.n

    def restart(self, base):
        self.base, self.n = base, 0


def hybrid_layer(nc, x, c, ada_w, ada_b, pre_mix_g, post_mix_g, pre_ffn_g, post_ffn_g,
                 w_in, lb_logits, gnorm_g, w_out, w_up, dw_w, dw_b, w_down, out):
    T, D = x.shape[1], x.shape[2]
    NT = T // P
    KD = D // P
    H = KD
    F = w_down.shape[1]
    FT = F // P
    TH = T // BANK
    LEVELS = 7
    AC = BANK
    JH = KD // 2
    START_PIECES = 2 * D // AC
    PIECES = 6 * D // AC
    assert T == 1024 and D == 1024 and FT * P == F and NT == 8 and TH == 2 and PIECES - START_PIECES == H

    x_rows = x.rearrange("b (n p) d -> (b n) p d", p=P)
    out_rows = out.rearrange("b (n p) d -> (b n) p d", p=P)
    ada_cols = ada_w.rearrange("l (j p) n -> p (l j) n", p=P)
    w_in_cols = w_in.rearrange("l (k p) n -> p (l k) n", p=P)
    w_out_rows = w_out.rearrange("l (k p) n -> (l k) p n", p=P)
    w_up_cols = w_up.rearrange("l (k p) n -> p (l k) n", p=P)
    w_down_rows = w_down.rearrange("l (k p) n -> (l k) p n", p=P)
    Q_COL, F_COL, I_COL, G_COL = 0, D, 2 * D, 3 * D
    x1_rows = nc.dram_tensor("x_after_mixer", (NT, P, D), F32, kind="Internal").ap()

    ctx = ExitStack()
    with ctx:
        def sb(name, shape, dt=F32, where=None):
            return (where or ctx).enter_context(nc.sbuf_tensor(name, shape, dt))

        def sem(name):
            return ctx.enter_context(nc.semaphore(name))

        ident = sb("ident", [P, P])
        ones = sb("ones", [P, P])
        level_mask = sb("level_mask", [P, LEVELS, P // 2])
        minus_half = sb("minus_half", [P, 8])
        VR = 5 * KD + 1
        vec_cols = sb("vec_cols", [P, VR])
        dw_cols = sb("dw_cols", [P, 4, 2 * FT])
        mix_scale = sb("mix_scale", [P, KD])
        mix_shift = sb("mix_shift", [P, KD])
        ffn_scale = sb("ffn_scale", [P, KD])
        ffn_shift = sb("ffn_shift", [P, KD])
        low = sb("low", [P, H])
        high = sb("high", [P, H])
        cond = sb("cond", [P, KD])
        tiny = sb("tiny", [P, 8, 8])
        stat = sb("stat", [P, 8, 8])
        mod_rows = sb("mod_rows", [P, 4, D])
        mod_flat = mod_rows[:, :, :].rearrange("p v d -> p (v d)")

        early = ExitStack()
        hT = sb("hT", [P, 2, KD, T], F32R, early)

        mixer = ExitStack()
        oT = sb("oT", [P, H, T], F32, mixer)
        head = ExitStack()
        w_raw = sb("w_raw", [P, 2, KD, P], F32, head)
        ada_raw = sb("ada_raw", [P, 2, JH, AC], F32, head)
        w_split = sb("w_split", [P, 2, 2, KD, P], F32R, head)
        late = ExitStack()
        f_dec = sb("f_dec", [P, T], F32, late)
        q_act = sb("q_act", [P, T], F32, late)
        gate = sb("gate", [P, T], F32, late)
        k_dec = sb("k_dec", [P, T], F32, late)
        totals = sb("totals", [P, T], F32, late)
        v_tok = sb("v_tok", [P, NT, P], F32, late)
        scores = sb("scores", [P, T], F32, late)
        q_dec = sb("q_dec", [P, T], F32, late)
        tok = sb("tok", [P, NT, P], F32, late)
        g_act = sb("g_act", [P, T], F32, late)
        states = sb("states", [P, NT - 1, P], F32, late)
        ada_acc = sb("ada_acc", [P, AC], F32, late)
        ada_bias = sb("ada_bias", [1, AC], F32, late)
        late.close()
        start = ExitStack()
        ada_more = sb("ada_more", [P, 3, JH, AC], F32, start)
        start.close()
        ada_slot = [ada_raw[:, 0], ada_raw[:, 1], ada_more[:, 0], ada_more[:, 1], ada_more[:, 2]]
        start_bias = mod_flat[0:1, 2 * D:4 * D]
        x_sb = oT
        vec_rows = tok[0:VR, 0, :]
        dw_rows = g_act[0:2 * FT, 0:4 * P].rearrange("n (t p) -> n t p", t=4)
        h_f32 = [q_dec, k_dec]
        head.close()

        project = ExitStack()
        slabs = sb("slabs", [P, 3, D], F32, project)
        WO_EARLY = 5
        wo_early = sb("wo_early", [P, WO_EARLY, 2, D], F32R, project)
        o_split = sb("o_split", [P, 2, 2, KD // 2, P], F32R, project)
        wo_late = sb("wo_late", [P, KD - WO_EARLY, 2, D], F32R, project)
        norm_tile = slabs[:, 0, :]

        def wo_split(k, part):
            return wo_early[:, k, part, :] if k < WO_EARLY else wo_late[:, k - WO_EARLY, part, :]

        project.close()
        mixer.close()

        up = ExitStack()
        up_split = sb("up_split", [P, 2, 2, KD, P], F32R, up)
        up_raw = sb("up_raw", [P, 2, KD, P], F32, up)
        act = sb("act", [P, FT, T], F32, up)
        conv_a, conv_b, sig_a = mod_rows[:, 0, :], mod_rows[:, 1, :], mod_rows[:, 2, :]
        up.close()
        early.close()

        down = ExitStack()
        a_split = sb("a_split", [P, 2, 2, T], F32R, down)
        wd_split = sb("wd_split", [P, 2, 2, BANK], F32R, down)
        wd_raw = sb("wd_raw", [P, 4, BANK], F32, down)
        y_left = sb("y_left", [P, NT, BANK], F32, down)
        x1_in = sb("x1_in", [P, 2, D], F32, down)
        out_sb = sb("out_sb", [P, 2, D], F32, down)
        down.close()

        ps = ctx.enter_context(nc.psum_tensor("ps", [P, 8, BANK], F32))

        def pair(n):
            return ps[:, 2 * n:2 * n + 2, :].rearrange("p a b -> p (a b)")

        vec_in = sem("vec_in")
        dw_in = sem("dw_in")
        x_in = [sem(f"x_in{i}") for i in range(NT)]
        w_in_arrived = [sem(f"w_in_arrived{s}") for s in range(2)]
        start_in = [sem(f"start_in{m}") for m in range(2 * START_PIECES)]
        start_bias_in = sem("start_bias_in")
        ada_in = [sem(f"ada_in{s}") for s in range(2)]
        post_in = sem("post_in")
        wo_in = [sem(f"wo_in{s}") for s in range(2)]
        xt_in = [sem(f"xt_in{u}") for u in range(2)]
        x1_stored = [sem(f"x1_stored{u}") for u in range(2)]
        up_in = [sem(f"up_in{s}") for s in range(2)]
        wd_in = [sem(f"wd_in{s}") for s in range(4)]
        x1_back = [sem(f"x1_back{u}") for u in range(2)]
        out_stored = [sem(f"out_stored{u}") for u in range(2)]

        pool_own = sem("pool_own")
        consts_made = sem("consts_made")
        rooted = sem("rooted")

        dve_own = sem("dve_own")
        act_own = sem("act_own")
        vecs_turned = sem("vecs_turned")
        dw_turned = sem("dw_turned")
        vecs_copied = sem("vecs_copied")
        lb_shifted = sem("lb_shifted")
        lb_exp = sem("lb_exp")
        c_sig = sem("c_sig")
        x_squared = sem("x_squared")
        x_mean = sem("x_mean")
        x_normed = sem("x_normed")
        x_turned = sem("x_turned")
        h_scaled = sem("h_scaled")
        h_split = sem("h_split")
        ada_used = sem("ada_used")
        ada_summed = sem("ada_summed")
        ada_spread = sem("ada_spread")
        ada_rowed = sem("ada_rowed")
        mod_turned = sem("mod_turned")
        mods_made = sem("mods_made")

        w_hi = sem("w_hi")
        w_lo = sem("w_lo")
        projected = sem("projected")
        sig_done = sem("sig_done")
        sig_used = sem("sig_used")
        values_copied = sem("values_copied")
        values_turned = sem("values_turned")
        v_ready = sem("v_ready")
        decayed = sem("decayed")
        scored = sem("scored")
        masked = sem("masked")
        keys_turned = sem("keys_turned")
        keys_ready = sem("keys_ready")
        chunk_kv = sem("chunk_kv")
        states_ready = sem("states_ready")
        o_ready = sem("o_ready")
        o_squared = sem("o_squared")
        o_mean = sem("o_mean")
        o_normed = sem("o_normed")
        o_turned = sem("o_turned")
        head_out = sem("head_out")

        wo_hi = sem("wo_hi")
        wo_lo = sem("wo_lo")
        o_hi = [sem(f"o_hi{q}") for q in range(2)]
        o_lo = [sem(f"o_lo{q}") for q in range(2)]
        o_used = [sem(f"o_used{q}") for q in range(2)]
        y_squared = sem("y_squared")
        y_mean = sem("y_mean")
        x1_made = sem("x1_made")
        x1_squared = sem("x1_squared")
        x1_mean = sem("x1_mean")
        x1_normed = sem("x1_normed")
        x1_turned = sem("x1_turned")
        h2_scaled = sem("h2_scaled")
        h2_split = sem("h2_split")

        up_hi = [sem(f"up_hi{s}") for s in range(2)]
        up_lo = [sem(f"up_lo{s}") for s in range(2)]
        upped = [sem(f"upped{s}") for s in range(2)]
        tap0 = [sem(f"tap0{s}") for s in range(2)]
        conved = [sem(f"conved{s}") for s in range(2)]
        a_sig = sem("a_sig")
        gated = sem("gated")

        a_hi = sem("a_hi")
        a_lo = sem("a_lo")
        wd_hi = sem("wd_hi")
        wd_lo = sem("wd_lo")
        downed = sem("downed")
        y_bank = sem("y_bank")
        out_squared = sem("out_squared")
        left_kept = sem("left_kept")
        out_mean = sem("out_mean")
        out_rooted = sem("out_rooted")
        out_made = sem("out_made")

        block = ctx.enter_context(nc.Block())

        @block.sync
        def _(sp):
            for i, rows in enumerate((c, pre_mix_g, pre_ffn_g)):
                sp.dma_start(vec_rows[i * KD:(i + 1) * KD, :],
                             rows.rearrange("a (k p) -> (a k) p", p=P)).then_inc(vec_in, 16)
            sp.dma_start(vec_rows[3 * KD:5 * KD, :],
                         lb_logits.rearrange("a (k p) -> (a k) p", p=P)).then_inc(vec_in, 16)
            sp.dma_start(vec_rows[5 * KD:VR, :], gnorm_g).then_inc(vec_in, 16)
            sp.dma_start(dw_rows[:, 0:3, :], dw_w.rearrange("a t (n p) -> n (a t) p", p=P)).then_inc(dw_in, 16)
            sp.dma_start(dw_rows[:, 3, :], dw_b.rearrange("a (n p) -> (a n) p", p=P)).then_inc(dw_in, 16)

            def load_w(n, col):
                sp.dma_start(w_raw[:, n % 2, :, :], w_in_cols[:, :, col]).then_inc(w_in_arrived[n % 2], 16)

            def load_piece(p, k):
                for s in range(2):
                    sp.wait_ge(ada_used, 2 * p - 1 + s)
                    sp.dma_start(ada_raw[:, s, :, :],
                                 ada_cols[:, s * JH:(s + 1) * JH, bass.ts(p, AC)]).then_inc(ada_in[s], 16)
                    if s == 1:
                        sp.wait_ge(ada_summed, p)
                        sp.dma_start(ada_bias[:, :], ada_b[:, bass.ts(p, AC)]).then_inc(ada_in[1], 16)

            for i in range(NT):
                sp.dma_start(x_sb[:, i, :], x_rows[i]).then_inc(x_in[i], 16)
            sp.dma_start(start_bias, ada_b[:, 0:2 * D]).then_inc(start_bias_in, 16)
            for m in range(2 * START_PIECES):
                if m >= len(ada_slot):
                    sp.wait_ge(ada_used, m - len(ada_slot) + 1)
                sp.dma_start(ada_slot[m % len(ada_slot)],
                             ada_cols[:, m % 2 * JH:(m % 2 + 1) * JH, m // 2 * AC:(m // 2 + 1) * AC]
                             ).then_inc(start_in[m], 16)
            load_w(0, slice(F_COL, F_COL + P))
            load_w(1, slice(Q_COL, Q_COL + P))
            sp.wait_ge(w_lo, 1)
            load_w(2, slice(I_COL, I_COL + P))
            sp.wait_ge(w_lo, 2)
            load_w(3, slice(G_COL, G_COL + P))
            load_piece(START_PIECES, 0)
            with sp.Fori(0, H - 1) as h:
                sp.wait_ge(w_lo, 4 * h + 3)
                load_w(0, bass.ds(F_COL + P + h * P, P))
                sp.wait_ge(w_lo, 4 * h + 4)
                load_w(1, bass.ds(Q_COL + P + h * P, P))
                load_piece(h + START_PIECES + 1, h + 1)
                sp.wait_ge(w_lo, 4 * h + 5)
                load_w(0, bass.ds(I_COL + P + h * P, P))
                sp.wait_ge(w_lo, 4 * h + 6)
                load_w(1, bass.ds(G_COL + P + h * P, P))

            sp.wait_ge(w_lo, 4 * H)
            sp.wait_ge(ada_summed, PIECES)
            for k in range(KD):
                if k >= 2:
                    sp.wait_ge(wo_lo, k - 1)
                sp.dma_start(slabs[:, 1 + k % 2, :], w_out_rows[k]).then_inc(wo_in[k % 2], 16)
                if k == 1:
                    sp.dma_start(slabs[:, 0, :], post_mix_g.broadcast_to((P, D))).then_inc(post_in, 16)
                if k == 3:
                    sp.wait_ge(mods_made, 2)
                    sp.dma_start(slabs[:, 0, :], post_ffn_g.broadcast_to((P, D))).then_inc(post_in, 16)
            sp.wait_ge(wo_lo, KD)
            sp.dma_start(slabs[:, 1, :], x_rows[0]).then_inc(xt_in[0], 16)
            sp.dma_start(slabs[:, 2, :], x_rows[1]).then_inc(xt_in[1], 16)
            with sp.Fori(0, NT // 2 - 1) as ii:
                for u in range(2):
                    sp.wait_ge(x1_made, 2 * ii + u + 1)
                    sp.dma_start(x1_rows[2 * ii + u], mod_rows[:, 1 + u, :]).then_inc(x1_stored[u], 16)
                    sp.dma_start(slabs[:, 1 + u, :], x_rows[2 * ii + u + 2]).then_inc(xt_in[u], 16)
            sp.wait_ge(o_lo[1], NT)
            sp.dma_start(up_raw[:, 0, :, :], w_up_cols[:, :, 0:P]).then_inc(up_in[0], 16)
            sp.dma_start(up_raw[:, 1, :, :], w_up_cols[:, :, F:F + P]).then_inc(up_in[1], 16)
            for u in range(2):
                sp.wait_ge(x1_made, NT - 1 + u)
                sp.dma_start(x1_rows[NT - 2 + u], mod_rows[:, 1 + u, :]).then_inc(x1_stored[u], 16)
            with sp.Fori(0, FT - 1) as j:
                for s in range(2):
                    sp.wait_ge(up_lo[s], j + 1)
                    sp.dma_start(up_raw[:, s, :, :],
                                 w_up_cols[:, :, bass.ds(s * F + P + j * P, P)]).then_inc(up_in[s], 16)

            sp.wait_ge(upped[1], FT)
            for kk in range(4):
                sp.dma_start(wd_raw[:, kk, :], w_down_rows[kk, :, 0:BANK]).then_inc(wd_in[kk], 16)
            for u in range(2):
                sp.wait_ge(x1_stored[u], 16 * NT // 2)
                sp.dma_start(x1_in[:, u, :], x1_rows[u]).then_inc(x1_back[u], 16)
            with sp.Fori(1, FT // 4) as m:
                for s in range(4):
                    sp.wait_ge(wd_lo, 4 * m + s - 3)
                    sp.dma_start(wd_raw[:, s, :], w_down_rows[4 * m + s, :, 0:BANK]).then_inc(wd_in[s], 16)
            for s in range(2):
                sp.wait_ge(wd_lo, FT + s - 5)
                sp.dma_start(wd_raw[:, s, :], w_down_rows[FT - 2 + s, :, 0:BANK]).then_inc(wd_in[s], 16)
            for s in range(2):
                sp.wait_ge(wd_lo, FT + s - 3)
                sp.dma_start(wd_raw[:, 2 + s, :], w_down_rows[s, :, BANK:D]).then_inc(wd_in[2 + s], 16)
            with sp.Fori(0, FT // 4) as m:
                for s in range(4):
                    sp.wait_ge(wd_lo, FT + 4 * m + s - 1)
                    sp.dma_start(wd_raw[:, s, :], w_down_rows[4 * m + s + 2, :, BANK:D]).then_inc(wd_in[s], 16)
            for t in range(NT):
                sp.wait_ge(out_made, t + 1)
                sp.dma_start(out_rows[t], out_sb[:, t % 2, :]).then_inc(out_stored[t % 2], 16)
                if t + 2 < NT:
                    sp.dma_start(x1_in[:, t % 2, :], x1_rows[t + 2]).then_inc(x1_back[t % 2], 16)
            for u in range(2):
                sp.wait_ge(out_stored[u], 16 * NT // 2)

        @block.gpsimd
        def _(pool):
            own = Tally()
            pool.memset(ident[:, :], 0.0).then_inc(pool_own, own.up())
            pool.memset(level_mask[:, :, :], 1.0).then_inc(pool_own, own.up())
            pool.memset(ones[:, :], 1.0).then_inc(consts_made, 1)
            pool.memset(minus_half[:, :], -0.5).then_inc(consts_made, 1)
            pool.wait_ge(pool_own, own.now)
            pool.affine_select(out=ident[:, :], in_=ident[:, :], compare_op=ALU.not_equal, fill=1.0, base=0,
                               pattern=[[-1, P]], channel_multiplier=1).then_inc(consts_made, 1)
            for j in range(LEVELS):
                half = 1 << j
                m = level_mask[:, j, :].rearrange("p (n w) -> p n w", w=half)
                blocks = P // (2 * half)
                pool.affine_select(out=m, in_=m, compare_op=ALU.is_ge, fill=0.0, base=0,
                                   pattern=[[-2 * half, blocks], [0, half]],
                                   channel_multiplier=1).then_inc(pool_own, own.up())
                pool.wait_ge(pool_own, own.now)
                pool.affine_select(out=m, in_=m, compare_op=ALU.is_ge, fill=0.0, base=half - 1,
                                   pattern=[[2 * half, blocks], [0, half]],
                                   channel_multiplier=-1).then_inc(consts_made, 1)
            pool.memset(scores[:, :], 0.0).then_inc(consts_made, 1)
            pool.wait_ge(consts_made, 2)
            pool.wait_ge(x_mean, 1)
            pool.tensor_tensor(stat[:, 0, :], tiny[:, 0, :], minus_half[:, :], ALU.pow).then_inc(rooted, 1)
            with pool.Fori(0, H) as h:
                pool.wait_ge(o_mean, h + 1)
                pool.tensor_tensor(stat[:, 1, :], tiny[:, 1, :], minus_half[:, :], ALU.pow).then_inc(rooted, 1)
            with pool.Fori(0, NT) as i:
                pool.wait_ge(y_mean, i + 1)
                pool.tensor_tensor(stat[:, 2, 0:1], tiny[:, 2, 0:1], minus_half[:, 0:1],
                                   ALU.pow).then_inc(rooted, 1)
                pool.wait_ge(x1_mean, i + 1)
                pool.tensor_tensor(stat[:, 3, 0:1], tiny[:, 3, 0:1], minus_half[:, 0:1],
                                   ALU.pow).then_inc(rooted, 1)
            for t in range(0, NT, 2):
                pool.wait_ge(out_mean, t // 2 + 1)
                pool.tensor_tensor(stat[:, 4, t:t + 2], tiny[:, 4, t:t + 2], minus_half[:, 0:2],
                                   ALU.pow).then_inc(out_rooted, 1)

        @block.scalar
        def _(sa):
            for i in range(NT):
                sa.wait_ge(x_in[i], 16)
                if i > 0:
                    sa.wait_ge(x_squared, i)
                sa.activation(pair(0), x_sb[:, i, :], ACT.Square,
                              accum_out=tiny[:, 5, i:i + 1]).then_inc(x_squared, 1)
            sa.wait_ge(lb_shifted, 1)
            sa.activation(stat[:, 5:7, :], stat[:, 5:7, :], ACT.Exp).then_inc(lb_exp, 1)
            sa.activation(cond[:, :], vec_cols[:, 0:KD], ACT.Sigmoid).then_inc(c_sig, 1)

            def split_w(n, s, load):
                sa.wait_ge(w_in_arrived[s], 16 * load)
                if not isinstance(n, int) or n >= 2:
                    sa.wait_ge(projected, n - 1)
                sa.activation(w_split[:, s, 0, :, :], w_raw[:, s, :, :], ACT.Copy).then_inc(w_hi, 1)

            def ada_row(p, dst):
                sa.wait_ge(ada_spread, p + 1)
                sa.activation(mod_flat[:, bass.ts(dst, AC)], ps[:, 6, :], ACT.Copy).then_inc(ada_rowed, 1)

            for p in range(START_PIECES):
                if p == START_PIECES - 1:
                    split_w(0, 0, 1)
                    split_w(1, 1, 1)
                ada_row(p, p)
            sa.wait_ge(mods_made, 1)
            for k in range(KD):
                sa.wait_ge(x_turned, k + 1)
                if k >= 2:
                    sa.wait_ge(h_split, k - 1)
                sa.activation(h_f32[k % 2][:, :], pair(k % 2), ACT.Identity, bias=mix_shift[:, k:k + 1],
                              scale=mix_scale[:, k:k + 1]).then_inc(h_scaled, 1)

            def sigmoid_f(h):
                sa.wait_ge(projected, 4 * h + 1)
                if not isinstance(h, int) or h > 0:
                    sa.wait_ge(sig_used, 3 * h)
                sa.activation(gate[:, :], pair(0), ACT.Sigmoid).then_inc(sig_done, 1)

            def head_front(h):
                sa.wait_ge(projected, 4 * h + 2)
                sa.wait_ge(sig_used, 3 * h + 1)
                sa.activation(gate[:, :], pair(1), ACT.Sigmoid).then_inc(sig_done, 1)
                split_w(4 * h + 3, 1, 2 * h + 2)
                sa.wait_ge(projected, 4 * h + 3)
                sa.wait_ge(sig_used, 3 * h + 2)
                sa.activation(gate[:, :], pair(0), ACT.Copy).then_inc(values_copied, 1)

            def head_values(h):
                sa.wait_ge(values_turned, h + 1)
                sa.activation(v_tok[:, :, :].rearrange("p n d -> p (n d)"), pair(3), ACT.Copy).then_inc(v_ready, 1)

            def sigmoid_g(h):
                sa.wait_ge(projected, 4 * h + 4)
                sa.activation(gate[:, :], pair(1), ACT.Sigmoid).then_inc(sig_done, 1)

            def head_keys(h):
                sa.wait_ge(keys_turned, h + 1)
                sa.activation(tok[:, :, :].rearrange("p n d -> p (n d)"), pair(3), ACT.Copy).then_inc(keys_ready, 1)

            def head_square(h):
                sa.wait_ge(o_ready, h + 1)
                sa.activation(tok[:, :, :].rearrange("p n d -> p (n d)"), pair(3), ACT.Square).then_inc(o_squared, 1)

            sigmoid_f(0)
            split_w(2, 0, 2)
            with sa.Fori(0, H - 1) as h:
                head_front(h)
                split_w(4 * h + 4, 0, 2 * h + 3)
                head_values(h)
                sigmoid_g(h)
                split_w(4 * h + 5, 1, 2 * h + 3)
                head_keys(h)
                ada_row(START_PIECES + h, h)
                sigmoid_f(h + 1)
                head_square(h)
                split_w(4 * h + 6, 0, 2 * h + 4)

            def split_wo(k):
                sa.wait_ge(wo_in[k % 2], 16 * (k // 2 + 1))
                sa.activation(wo_split(k, 0), slabs[:, 1 + k % 2, :], ACT.Copy).then_inc(wo_hi, 1)

            head_front(H - 1)
            split_wo(0)
            head_values(H - 1)
            split_wo(1)
            sigmoid_g(H - 1)
            split_wo(2)
            head_keys(H - 1)
            split_wo(3)
            ada_row(PIECES - 1, H - 1)
            sa.wait_ge(sig_used, 3 * H)
            split_wo(4)
            head_square(H - 1)

            def split_o(i, q):
                if not isinstance(i, int) or i > 0:
                    sa.wait_ge(o_used[q], i)
                sa.activation(o_split[:, q, 0, :, :],
                              oT[:, q * (KD // 2):(q + 1) * (KD // 2), bass.ts(i, P)],
                              ACT.Copy).then_inc(o_hi[q], 1)

            def square_y(i, u):
                sa.wait_ge(o_used[1], i + 1)
                sa.activation(pair(3), pair(u), ACT.Square, accum_out=tiny[:, 6, 0:1]).then_inc(y_squared, 1)

            def scale_h2(i):
                sa.wait_ge(x1_turned, i + 1)
                for k in range(KD):
                    done = sa.activation(norm_tile[:, k * P:(k + 1) * P], pair(2)[:, k * P:(k + 1) * P],
                                         ACT.Identity, bias=ffn_shift[:, k:k + 1], scale=ffn_scale[:, k:k + 1])
                done.then_inc(h2_scaled, 1)

            def norm_x1(i, u):
                sa.wait_ge(x1_made, i + 1)
                sa.activation(pair(3), mod_rows[:, 1 + u, :], ACT.Square,
                              accum_out=tiny[:, 7, 0:1]).then_inc(x1_squared, 1)
                if not isinstance(i, int) or i > 0:
                    sa.wait_ge(h2_split, i)
                sa.wait_ge(rooted, 1 + H + 2 * i + 2)
                sa.activation(norm_tile, mod_rows[:, 1 + u, :], ACT.Copy,
                              scale=stat[:, 3, 0:1]).then_inc(x1_normed, 1)

            split_o(0, 0)
            split_wo(5)
            sa.wait_ge(o_turned, H)
            split_wo(6)
            sa.wait_ge(head_out, H)
            split_o(0, 1)
            split_wo(7)
            sa.wait_ge(mods_made, 4)
            split_o(1, 0)
            square_y(0, 0)
            split_o(1, 1)
            norm_x1(0, 0)

            def mixer_tile(i, u):
                split_o(i + 1, 0)
                square_y(i, u)
                split_o(i + 1, 1)
                scale_h2(i - 1)
                norm_x1(i, u)

            mixer_tile(1, 1)
            with sa.Fori(1, NT // 2 - 1) as ii:
                for u in range(2):
                    mixer_tile(2 * ii + u, u)
            mixer_tile(NT - 2, 0)

            def split_up(j, s):
                sa.wait_ge(up_in[s], 16 * (j + 1))
                if not isinstance(j, int) or j > 0:
                    sa.wait_ge(upped[s], j)
                sa.activation(up_split[:, s, 0, :, :], up_raw[:, s, :, :], ACT.Copy).then_inc(up_hi[s], 1)

            sa.wait_ge(o_lo[1], NT)
            split_up(0, 0)
            split_up(0, 1)
            square_y(NT - 1, 1)
            scale_h2(NT - 2)
            norm_x1(NT - 1, 1)
            scale_h2(NT - 1)

            def first_tap(j, s, dst):
                ft = j + s * FT
                sa.wait_ge(upped[s], j + 1)
                if not isinstance(j, int) or j > 0:
                    sa.wait_ge(gated, j)
                sa.activation(dst, pair(s), ACT.Identity, bias=dw_cols[:, 3, bass.ds(ft, 1)],
                              scale=dw_cols[:, 2, bass.ds(ft, 1)]).then_inc(tap0[s], 1)

            def sigmoid_a(j):
                sa.wait_ge(conved[0], j + 1)
                sa.activation(sig_a, conv_a, ACT.Sigmoid).then_inc(a_sig, 1)

            for u in range(2):
                sa.wait_ge(x1_stored[u], 16 * NT // 2)
            first_tap(0, 0, conv_a)
            split_up(1, 0)
            sigmoid_a(0)
            first_tap(0, 1, conv_b)
            split_up(1, 1)
            with sa.Fori(1, FT - 1) as j:
                first_tap(j, 0, conv_a)
                split_up(j + 1, 0)
                sigmoid_a(j)
                first_tap(j, 1, conv_b)
                split_up(j + 1, 1)
            first_tap(FT - 1, 0, conv_a)
            sigmoid_a(FT - 1)

            def split_down(kk, k, r, load, freed=lambda kk: kk - 1):
                s = r % 2
                if freed:
                    sa.wait_ge(downed, freed(kk))
                sa.activation(a_split[:, s, 0, :], act[:, k, :], ACT.Copy).then_inc(a_hi, 1)
                sa.wait_ge(wd_in[r], 16 * load)
                sa.activation(wd_split[:, s, 0, :], wd_raw[:, r, :], ACT.Copy).then_inc(wd_hi, 1)

            def square_out(half, t):
                sa.wait_ge(y_bank, half * NT + t + 1)
                sa.activation(y_left[:, t, :] if half == 0 else out_sb[:, t % 2, 0:BANK], ps[:, t, :], ACT.Square,
                              accum_out=tiny[:, half, t:t + 1]).then_inc(out_squared, 1)

            sa.wait_ge(upped[1], FT)
            sa.wait_ge(gated, 2)
            split_down(0, 0, 0, 1, None)
            split_down(1, 1, 1, 1, None)
            first_tap(FT - 1, 1, conv_b)
            split_down(2, 2, 2, 1)
            split_down(3, 3, 3, 1)
            with sa.Fori(1, FT // 4) as m:
                for r in range(4):
                    split_down(4 * m + r, 4 * m + r, r, m + 1)
            sa.wait_ge(gated, FT)
            split_down(FT - 2, FT - 2, 0, FT // 4 + 1)
            split_down(FT - 1, FT - 1, 1, FT // 4 + 1)
            split_down(FT, 0, 2, FT // 4 + 1)
            for t in range(NT):
                square_out(0, t)
            split_down(FT + 1, 1, 3, FT // 4 + 1, None)
            with sa.Fori(0, FT // 4) as m:
                for r in range(4):
                    split_down(FT + 2 + 4 * m + r, 4 * m + r + 2, r, m + (FT // 4 + 2),
                               lambda kk: kk - 2)
            for t in range(NT):
                if t >= 2:
                    sa.wait_ge(out_stored[t % 2], 16 * (t // 2))
                square_out(1, t)

        @block.vector
        def _(ve):
            own = Tally()

            def link(ins):
                ins.then_inc(dve_own, own.up())
                ve.wait_ge(dve_own, own.now)

            ve.wait_ge(vecs_turned, 1)
            ve.tensor_copy(vec_cols[:, :], ps[:, 4, 0:VR]).then_inc(vecs_copied, 1)
            ve.wait_ge(vecs_copied, 1)
            l0, l1 = vec_cols[:, 3 * KD:4 * KD], vec_cols[:, 4 * KD:5 * KD]
            e0, e1 = stat[:, 5, :], stat[:, 6, :]
            link(ve.tensor_tensor(stat[:, 7, :], l0, l1, ALU.max))
            ve.tensor_tensor(e0, l0, stat[:, 7, :], ALU.subtract)
            ve.tensor_tensor(e1, l1, stat[:, 7, :], ALU.subtract).then_inc(lb_shifted, 1)
            ve.wait_ge(dw_turned, 1)
            ve.tensor_copy(dw_cols[:, :, :].rearrange("p t n -> p (t n)"), ps[:, 5, 0:8 * FT]).then_inc(vecs_copied, 1)
            ve.wait_ge(lb_exp, 1)
            link(ve.tensor_tensor(stat[:, 7, :], e0, e1, ALU.add))
            link(ve.reciprocal(stat[:, 7, :], stat[:, 7, :]))
            link(ve.tensor_tensor(low[:, :], e0, stat[:, 7, :], ALU.mult))
            ve.tensor_scalar(high[:, :], low[:, :], -1.0, 1.0, ALU.mult, ALU.add)
            ve.wait_ge(c_sig, 1)
            link(ve.tensor_tensor(cond[:, :], cond[:, :], vec_cols[:, 0:KD], ALU.mult))

            ve.wait_ge(x_squared, NT)
            ve.tensor_scalar(tiny[:, 0, :], tiny[:, 5, :], 1.0 / D, EPS, ALU.mult, ALU.add).then_inc(x_mean, 1)
            ve.wait_ge(rooted, 1)
            for i in range(NT):
                ve.tensor_scalar(x_sb[:, i, :], x_sb[:, i, :], stat[:, 0, i:i + 1], None,
                                 ALU.mult).then_inc(x_normed, 1)

            def split_w(n, s):
                ve.wait_ge(w_hi, n + 1)
                ve.tensor_tensor(w_split[:, s, 1, :, :], w_raw[:, s, :, :], w_split[:, s, 0, :, :].bitcast(F32),
                                 ALU.subtract).then_inc(w_lo, 1)

            def ada_piece(p):
                acc = ada_acc[:, :]
                for s in range(2):
                    ve.wait_ge(ada_in[s], 16 * (s + 1) * (p + (1 - START_PIECES)))
                    for j in range(JH):
                        k = s * JH + j
                        if k == 0:
                            ve.wait_ge(ada_spread, p)
                            ins = ve.tensor_scalar(acc, ada_raw[:, s, j, :], cond[:, k:k + 1], None, ALU.mult)
                        else:
                            ins = ve.scalar_tensor_tensor(out=acc, in0=ada_raw[:, s, j, :], scalar=cond[:, k:k + 1],
                                                          in1=acc, op0=ALU.mult, op1=ALU.add)
                        if j == JH - 1:
                            ins.then_inc(ada_used, 1)
                            ve.wait_ge(ada_used, 2 * p + s + 1)
                        else:
                            link(ins)
                ve.tensor_tensor(ada_acc[0:1, :], ada_acc[0:1, :], ada_bias[:, :], ALU.add).then_inc(ada_summed, 1)

            def start_piece(p):
                acc = ada_acc[:, :]
                for s in range(2):
                    m = 2 * p + s
                    ve.wait_ge(start_in[m], 16)
                    for j in range(JH):
                        k = s * JH + j
                        src = ada_slot[m % len(ada_slot)][:, j, :]
                        if k == 0:
                            if p > 0:
                                ve.wait_ge(ada_spread, p)
                            ins = ve.tensor_scalar(acc, src, cond[:, k:k + 1], None, ALU.mult)
                        else:
                            ins = ve.scalar_tensor_tensor(out=acc, in0=src, scalar=cond[:, k:k + 1],
                                                          in1=acc, op0=ALU.mult, op1=ALU.add)
                        if j == JH - 1:
                            ins.then_inc(ada_used, 1)
                            ve.wait_ge(ada_used, m + 1)
                        else:
                            link(ins)
                if p == 0:
                    ve.wait_ge(start_bias_in, 16)
                ve.tensor_tensor(ada_acc[0:1, :], ada_acc[0:1, :], start_bias[:, p * AC:(p + 1) * AC],
                                 ALU.add).then_inc(ada_summed, 1)

            for p in range(START_PIECES):
                if p > 0:
                    ve.wait_ge(ada_summed, p)
                if p == START_PIECES - 1:
                    split_w(0, 0)
                    split_w(1, 1)
                start_piece(p)

            def modulation(shift, scale, gain):
                ve.tensor_copy(shift[:, :], ps[:, 7, 0:KD])
                return ve.scalar_tensor_tensor(out=scale[:, :], in0=ps[:, 7, KD:2 * KD], scalar=1.0, in1=gain,
                                               op0=ALU.add, op1=ALU.mult)

            ve.wait_ge(mod_turned, 1)
            modulation(mix_shift, mix_scale, vec_cols[:, KD:2 * KD]).then_inc(mods_made, 1)
            for k in range(KD):
                ve.wait_ge(h_scaled, k + 1)
                link(ve.tensor_copy(hT[:, 0, k, :], h_f32[k % 2][:, :]))
                ve.tensor_tensor(hT[:, 1, k, :], h_f32[k % 2][:, :], hT[:, 0, k, :].bitcast(F32),
                                 ALU.subtract).then_inc(h_split, 1)

            def forget(h):
                ve.wait_ge(sig_done, 3 * h + 1)
                ve.tensor_scalar(f_dec[:, :], gate[:, :], high[:, bass.ds(h, 1)], low[:, bass.ds(h, 1)],
                                 ALU.mult, ALU.add).then_inc(sig_used, 1)

            def mask(n, bank_n):
                if n == 0:
                    ve.copy_predicated(scores[:, :].rearrange("p (c t) -> p c t", t=P),
                                       ident[:, :].bitcast(I32).unsqueeze(1).broadcast_to((P, NT, P)),
                                       pair(2).rearrange("p (c t) -> p c t", t=P)).then_inc(masked, 1)
                    return
                half = 1 << (n - 1)
                ve.copy_predicated(
                    scores[:, :].rearrange("p (n two w) -> p n two w", two=2, w=half)[:, :, 1, :],
                    level_mask[:, n - 1, :].bitcast(I32).unsqueeze(1).broadcast_to((P, NT, P // 2)),
                    ps[:, bank_n, :].rearrange("p (n w) -> p n w", w=half)).then_inc(masked, 1)

            TOTAL_AT = [None, 0] + [T - (T >> (j - 1)) for j in range(2, LEVELS + 1)]

            def total(j):
                n = T >> j
                return f_dec[:, :] if j == 0 else totals[:, TOTAL_AT[j]:TOTAL_AT[j] + n]

            def take_level(h, n):
                j = n - 1
                half = 1 << j
                tj = total(j).rearrange("p (n two) -> p n two", two=2)
                blocks = T // (2 * half)
                right = q_dec[:, :].rearrange("p (n two w) -> p n two w", two=2, w=half)[:, :, 1, :]
                left = k_dec[:, :].rearrange("p (n two w) -> p n two w", two=2, w=half)[:, :, 0, :]
                ve.wait_ge(decayed, 8 * h + n)
                ve.wait_ge(scored, 8 * h + n + 1)
                if n > 1:
                    ve.wait_ge(masked, 8 * h + n)
                ve.tensor_tensor(total(j + 1).unsqueeze(2), tj[:, :, 0:1], tj[:, :, 1:2], ALU.mult)
                if n == 1:
                    mask(0, None)
                    ve.wait_ge(masked, 8 * h + 1)
                ve.tensor_tensor(right, right, tj[:, :, 0:1].broadcast_to((P, blocks, half)), ALU.mult)
                ve.tensor_tensor(left, left, tj[:, :, 1:2].broadcast_to((P, blocks, half)),
                                 ALU.mult).then_inc(decayed, 1)
                mask(n, level_bank[n])

            level_bank = [None, 6, 7, 4, 5, 4, 5, 4]

            def head_start(h):
                ve.wait_ge(sig_used, 3 * h + 1)
                ve.tensor_scalar(k_dec[:, :], f_dec[:, :], -1.0, 1.0, ALU.mult, ALU.add)
                ve.wait_ge(sig_done, 3 * h + 2)
                ve.tensor_tensor(q_act[:, :], pair(1), gate[:, :], ALU.mult).then_inc(sig_used, 1)
                ve.wait_ge(sig_used, 3 * h + 2)
                ve.tensor_tensor(q_dec[:, :], q_act[:, :], f_dec[:, :], ALU.mult).then_inc(decayed, 1)
                split_w(4 * h + 3, 1)
                for n in (1, 2):
                    take_level(h, n)

            def gate_out(h):
                ve.wait_ge(sig_done, 3 * h + 3)
                ve.tensor_tensor(g_act[:, :], pair(1), gate[:, :], ALU.mult).then_inc(sig_used, 1)

            def head_states(h):
                tot = total(LEVELS)
                kv = pair(2).rearrange("p (c d) -> p c d", d=P)
                ve.wait_ge(chunk_kv, h + 1)
                link(ve.tensor_copy(states[:, 0, :], kv[:, 0, :]))
                for ch in range(1, NT - 1):
                    ins = ve.scalar_tensor_tensor(out=states[:, ch, :], in0=states[:, ch - 1, :],
                                                  scalar=tot[:, ch:ch + 1], in1=kv[:, ch, :],
                                                  op0=ALU.mult, op1=ALU.add)
                    if ch < NT - 2:
                        link(ins)
                ins.then_inc(states_ready, 1)

            def head_norm(h):
                o = pair(3).rearrange("p (c d) -> p c d", d=P)
                ve.wait_ge(o_squared, h + 1)
                link(ve.reduce_sum(tiny[:, 2, :], tok[:, :, :], axis=AX_X))
                ve.tensor_scalar(tiny[:, 1, :], tiny[:, 2, :], 1.0 / P, EPS, ALU.mult, ALU.add).then_inc(o_mean, 1)
                ve.wait_ge(rooted, h + 2)
                ve.tensor_tensor(tok[:, :, :], o, stat[:, 1, :].unsqueeze(2).broadcast_to((P, NT, P)),
                                 ALU.mult).then_inc(o_normed, 1)

            def head_end(h):
                ve.wait_ge(o_turned, h + 1)
                ve.wait_ge(sig_used, 3 * h + 3)
                ve.scalar_tensor_tensor(out=oT[:, h, :], in0=pair(2), scalar=vec_cols[:, 5 * KD:VR],
                                        in1=g_act[:, :], op0=ALU.mult, op1=ALU.mult).then_inc(head_out, 1)

            forget(0)
            split_w(2, 0)
            ve.wait_ge(ada_summed, START_PIECES)
            ada_piece(START_PIECES)
            base, per = own.now, (NT - 2) + 1 + 2 * (JH - 1)
            with ve.Fori(0, H - 1) as h:
                own.restart(base + h * per)
                head_start(h)
                split_w(4 * h + 4, 0)
                for n in range(3, LEVELS + 1):
                    take_level(h, n)
                gate_out(h)
                split_w(4 * h + 5, 1)
                head_states(h)
                forget(h + 1)
                head_norm(h)
                split_w(4 * h + 6, 0)
                head_end(h)
                ve.wait_ge(ada_summed, START_PIECES + h + 1)
                ada_piece(START_PIECES + h + 1)
                assert own.n == per
            own.restart(base + (H - 1) * per)
            last = H - 1

            def split_wo(k):
                ve.wait_ge(wo_hi, k + 1)
                ve.tensor_tensor(wo_split(k, 1), slabs[:, 1 + k % 2, :], wo_split(k, 0).bitcast(F32),
                                 ALU.subtract).then_inc(wo_lo, 1)

            def split_o(i, q):
                ve.wait_ge(o_hi[q], i + 1)
                ve.tensor_tensor(o_split[:, q, 1, :, :],
                                 oT[:, q * (KD // 2):(q + 1) * (KD // 2), bass.ts(i, P)],
                                 o_split[:, q, 0, :, :].bitcast(F32), ALU.subtract).then_inc(o_lo[q], 1)

            head_start(last)
            for n in range(3, LEVELS + 1):
                take_level(last, n)
                if n == 4:
                    split_wo(0)
                if n == 5:
                    ve.wait_ge(post_in, 16)
                    ve.tensor_tensor(mod_rows[:, 0, :], mod_rows[:, 0, :], slabs[:, 0, :],
                                     ALU.mult).then_inc(mods_made, 1)
                if n == 6:
                    split_wo(1)
            gate_out(last)
            split_wo(2)
            head_states(last)
            ve.wait_ge(mod_turned, 2)
            modulation(ffn_shift, ffn_scale, vec_cols[:, 2 * KD:3 * KD]).then_inc(mods_made, 1)
            split_wo(3)
            head_norm(last)
            split_o(0, 0)
            split_wo(4)
            ve.wait_ge(post_in, 32)
            ve.wait_ge(ada_rowed, PIECES)
            ve.tensor_tensor(mod_rows[:, 3, :], mod_rows[:, 3, :], slabs[:, 0, :], ALU.mult).then_inc(mods_made, 1)
            head_end(last)

            def make_x1(i, u, times):
                x1 = mod_rows[:, 1 + u, :]
                ve.wait_ge(y_squared, i + 1)
                ve.tensor_scalar(tiny[:, 2, 0:1], tiny[:, 6, 0:1], 1.0 / D, EPS,
                                 ALU.mult, ALU.add).then_inc(y_mean, 1)
                if not isinstance(times, int) or times > 0:
                    ve.wait_ge(x1_stored[u], 16 * times)
                ve.wait_ge(rooted, 1 + H + 2 * i + 1)
                link(ve.scalar_tensor_tensor(out=x1, in0=pair(u), scalar=stat[:, 2, 0:1], in1=mod_rows[:, 0, :],
                                             op0=ALU.mult, op1=ALU.mult))
                ve.wait_ge(xt_in[u], 16 * (times + 1))
                ve.tensor_tensor(x1, x1, slabs[:, 1 + u, :], ALU.add).then_inc(x1_made, 1)

            def mean_x1(i):
                ve.wait_ge(x1_squared, i + 1)
                ve.tensor_scalar(tiny[:, 3, 0:1], tiny[:, 7, 0:1], 1.0 / D, EPS,
                                 ALU.mult, ALU.add).then_inc(x1_mean, 1)

            def split_h2(i):
                h2 = norm_tile.rearrange("p (k t) -> p k t", t=P)
                hi, lo = hT[:, 0, :, bass.ts(i, P)], hT[:, 1, :, bass.ts(i, P)]
                ve.wait_ge(h2_scaled, i + 1)
                link(ve.tensor_copy(hi, h2))
                ve.tensor_tensor(lo, h2, hi.bitcast(F32), ALU.subtract).then_inc(h2_split, 1)

            split_wo(5)
            split_wo(6)
            split_o(0, 1)
            split_wo(7)
            split_o(1, 0)
            make_x1(0, 0, 0)
            split_o(1, 1)
            mean_x1(0)

            def mixer_tile(i, u, times):
                split_o(i + 1, 0)
                make_x1(i, u, times)
                split_o(i + 1, 1)
                split_h2(i - 1)
                mean_x1(i)

            mixer_tile(1, 1, 0)
            base, per = own.now, 4
            with ve.Fori(1, NT // 2 - 1) as ii:
                own.restart(base + (ii - 1) * per)
                for u in range(2):
                    mixer_tile(2 * ii + u, u, ii)
                assert own.n == per
            own.restart(base + (NT // 2 - 2) * per)
            mixer_tile(NT - 2, 0, NT // 2 - 1)

            def split_up(j, s):
                ve.wait_ge(up_hi[s], j + 1)
                ve.tensor_tensor(up_split[:, s, 1, :, :], up_raw[:, s, :, :],
                                 up_split[:, s, 0, :, :].bitcast(F32), ALU.subtract).then_inc(up_lo[s], 1)

            split_up(0, 0)
            split_up(0, 1)
            make_x1(NT - 1, 1, NT // 2 - 1)
            split_h2(NT - 2)
            mean_x1(NT - 1)
            split_h2(NT - 1)

            def more_taps(j, s, dst):
                ft = j + s * FT
                ve.wait_ge(tap0[s], j + 1)
                link(ve.scalar_tensor_tensor(out=dst[:, 1:T], in0=pair(s)[:, 0:T - 1],
                                             scalar=dw_cols[:, 1, bass.ds(ft, 1)], in1=dst[:, 1:T],
                                             op0=ALU.mult, op1=ALU.add))
                ve.scalar_tensor_tensor(out=dst[:, 2:T], in0=pair(s)[:, 0:T - 2],
                                        scalar=dw_cols[:, 0, bass.ds(ft, 1)], in1=dst[:, 2:T],
                                        op0=ALU.mult, op1=ALU.add).then_inc(conved[s], 1)

            def gate_ffn(j):
                ve.wait_ge(conved[1], j + 1)
                link(ve.tensor_tensor(conv_b, conv_b, conv_a, ALU.mult))
                ve.wait_ge(a_sig, j + 1)
                ve.tensor_tensor(act[:, j, :], conv_b, sig_a, ALU.mult).then_inc(gated, 1)

            base, per = own.now, 3
            with ve.Fori(0, FT - 1) as j:
                own.restart(base + j * per)
                more_taps(j, 0, conv_a)
                split_up(j + 1, 0)
                more_taps(j, 1, conv_b)
                split_up(j + 1, 1)
                gate_ffn(j)
                assert own.n == per
            own.restart(base + (FT - 1) * per)
            more_taps(FT - 1, 0, conv_a)

            def split_down(kk, k, r):
                s = r % 2
                ve.wait_ge(a_hi, kk + 1)
                ve.tensor_tensor(a_split[:, s, 1, :], act[:, k, :], a_split[:, s, 0, :].bitcast(F32),
                                 ALU.subtract).then_inc(a_lo, 1)
                ve.wait_ge(wd_hi, kk + 1)
                ve.tensor_tensor(wd_split[:, s, 1, :], wd_raw[:, r, :], wd_split[:, s, 0, :].bitcast(F32),
                                 ALU.subtract).then_inc(wd_lo, 1)

            split_down(0, 0, 0)
            split_down(1, 1, 1)
            more_taps(FT - 1, 1, conv_b)
            gate_ffn(FT - 1)
            split_down(2, 2, 2)
            split_down(3, 3, 3)
            with ve.Fori(1, FT // 4) as m:
                for r in range(4):
                    split_down(4 * m + r, 4 * m + r, r)
            split_down(FT - 2, FT - 2, 0)
            split_down(FT - 1, FT - 1, 1)
            split_down(FT, 0, 2)
            g2 = mod_rows[:, 3, :]
            for t in range(NT):
                ve.wait_ge(out_squared, t + 1)
                ve.tensor_tensor(y_left[:, t, :], ps[:, t, :], g2[:, 0:BANK], ALU.mult).then_inc(left_kept, 1)
            split_down(FT + 1, 1, 3)
            with ve.Fori(0, FT // 4) as m:
                for r in range(4):
                    split_down(FT + 2 + 4 * m + r, 4 * m + r + 2, r)

            def finish(t):
                o, x1 = out_sb[:, t % 2, :], x1_in[:, t % 2, :]
                ve.wait_ge(out_rooted, t // 2 + 1)
                ve.wait_ge(x1_back[t % 2], 16 * (t // 2 + 1))
                ve.scalar_tensor_tensor(out=o[:, 0:BANK], in0=y_left[:, t, :], scalar=stat[:, 4, t:t + 1],
                                        in1=x1[:, 0:BANK], op0=ALU.mult, op1=ALU.add)
                ve.scalar_tensor_tensor(out=o[:, BANK:D], in0=o[:, BANK:D], scalar=stat[:, 4, t:t + 1],
                                        in1=x1[:, BANK:D], op0=ALU.mult, op1=ALU.add).then_inc(out_made, 1)

            for t in range(0, NT, 2):
                for u in range(2):
                    ve.wait_ge(out_squared, NT + t + u + 1)
                    ve.tensor_tensor(out_sb[:, u, BANK:D], ps[:, t + u, :], g2[:, BANK:D], ALU.mult)
                link(ve.tensor_tensor(tiny[:, 5, t:t + 2], tiny[:, 0, t:t + 2], tiny[:, 1, t:t + 2], ALU.add))
                ve.tensor_scalar(tiny[:, 4, t:t + 2], tiny[:, 5, t:t + 2], 1.0 / D, EPS,
                                 ALU.mult, ALU.add).then_inc(out_mean, 1)
                for u in range(2):
                    finish(t + u)

        @block.tensor
        def _(pe):
            HI, LO = 0, 1
            PARTS = ((HI, HI), (HI, LO), (LO, HI))

            def turn(dst, src, n=P):
                return pe.transpose(dst, src, ident[0:n, 0:n])

            pe.wait_ge(consts_made, 3 + LEVELS + 1)
            pe.wait_ge(vec_in, 16 * 5)
            turn(ps[:, 4, 0:VR], vec_rows, VR).then_inc(vecs_turned, 1)
            pe.wait_ge(dw_in, 32)
            for t in range(4):
                last = turn(ps[:, 5, 2 * FT * t:2 * FT * (t + 1)], dw_rows[:, t, :], 2 * FT)
            last.then_inc(dw_turned, 1)

            def spread(p):
                pe.wait_ge(ada_summed, p + 1)
                if not isinstance(p, int) or p > 0:
                    pe.wait_ge(ada_rowed, p)
                pe.matmul(ps[:, 6, :], ones[:, :], ada_acc[:, :], start=True, stop=True).then_inc(ada_spread, 1)

            def turn_mods(row):
                for v in range(2):
                    for k in range(KD):
                        last = turn(ps[:, 7, v * KD + k:v * KD + k + 1],
                                    mod_rows[0:1, row + v, k * P:(k + 1) * P], 1)
                last.then_inc(mod_turned, 1)

            for p in range(START_PIECES):
                spread(p)
            pe.wait_ge(ada_rowed, START_PIECES)
            pe.wait_ge(vecs_copied, 2)
            turn_mods(0)
            pe.wait_ge(x_normed, NT)
            for k in range(KD):
                if k >= 2:
                    pe.wait_ge(h_scaled, k - 1)
                for i in range(NT):
                    last = turn(pair(k % 2)[:, i * P:(i + 1) * P], x_sb[:, i, k * P:(k + 1) * P])
                last.then_inc(x_turned, 1)

            def project_quarter(s, half, kh, done=None):
                for k in range(kh * (KD // 2), (kh + 1) * (KD // 2)):
                    for n, (a, b) in enumerate(PARTS):
                        last = pe.matmul(ps[:, 2 * s + half, :], w_split[:, s, a, k, :],
                                         hT[:, b, k, half * BANK:(half + 1) * BANK],
                                         start=(k == 0 and n == 0), stop=(k == KD - 1 and n == 2))
                if done is not None:
                    last.then_inc(done, 1)

            def group(s, quarter, n, freed=None, count=None):
                if quarter == 0:
                    pe.wait_ge(w_lo, n + 1)
                    if freed is not None:
                        pe.wait_ge(freed, count)
                project_quarter(s, quarter // 2, quarter % 2, projected if quarter == 3 else None)

            def chunk(ap, ch):
                return ap[:, ch * P:(ch + 1) * P]

            def diagonal(h):
                pe.wait_ge(decayed, 8 * h + 1)
                for ch in range(NT):
                    last = pe.matmul(chunk(pair(2), ch), chunk(k_dec, ch), chunk(q_act, ch), start=True, stop=True)
                last.then_inc(scored, 1)

            def level(h, n, bank_n, masked_n=None):
                half = 1 << (n - 1)
                pe.wait_ge(decayed, 8 * h + n)
                if masked_n is not None:
                    pe.wait_ge(masked, 8 * h + masked_n)
                for ch in range(NT):
                    moving = chunk(q_dec, ch).rearrange("p (n two w) -> p n two w", two=2, w=half)[:, :, 1, :]
                    last = pe.matmul(ps[:, bank_n, ch * (P // 2):(ch + 1) * (P // 2)], chunk(k_dec, ch), moving,
                                     start=True, stop=True)
                last.then_inc(scored, 1)

            def turn_values(h):
                pe.wait_ge(values_copied, h + 1)
                pe.wait_ge(masked, 8 * h + 3)
                for ch in range(NT):
                    last = turn(chunk(pair(3), ch), chunk(gate, ch))
                last.then_inc(values_turned, 1)

            def turn_keys(h):
                pe.wait_ge(decayed, 8 * h + 8)
                pe.wait_ge(v_ready, h + 1)
                for ch in range(NT):
                    last = turn(chunk(pair(3), ch), chunk(k_dec, ch))
                last.then_inc(keys_turned, 1)

            def keys_values(h):
                pe.wait_ge(keys_ready, h + 1)
                pe.wait_ge(masked, 8 * h + 8)
                for ch in range(NT - 1):
                    last = pe.matmul(chunk(pair(2), ch), tok[:, ch, :], v_tok[:, ch, :], start=True, stop=True)
                last.then_inc(chunk_kv, 1)

            def outputs(h):
                pe.wait_ge(ada_rowed, START_PIECES + h + 1)
                pe.wait_ge(states_ready, h + 1)
                for ch in range(NT):
                    last = pe.matmul(chunk(pair(3), ch), chunk(scores, ch), v_tok[:, ch, :],
                                     start=True, stop=(ch == 0))
                    if ch > 0:
                        last = pe.matmul(chunk(pair(3), ch), chunk(q_dec, ch), states[:, ch - 1, :],
                                         start=False, stop=True)
                last.then_inc(o_ready, 1)

            def turn_outputs(h):
                pe.wait_ge(o_normed, h + 1)
                for ch in range(NT):
                    last = turn(chunk(pair(2), ch), tok[:, ch, :])
                last.then_inc(o_turned, 1)

            pe.wait_ge(w_lo, 1)
            for quarter in range(4):
                if quarter < 2:
                    pe.wait_ge(h_split, KD // 2 * (quarter + 1))
                if quarter == 0:
                    pe.wait_ge(h_scaled, KD)
                group(0, quarter, 0)
            for quarter in range(4):
                group(1, quarter, 1)

            def head_first_half(h):
                for quarter in range(4):
                    group(0, quarter, 4 * h + 2, sig_done, 3 * h + 1)
                    if quarter == 1:
                        diagonal(h)
                        level(h, 1, 6)
                    if quarter == 2:
                        level(h, 2, 7)
                    if quarter == 3:
                        level(h, 3, 4, 1)
                for quarter in range(4):
                    group(1, quarter, 4 * h + 3, sig_used, 3 * h + 2)
                    if quarter == 0:
                        turn_values(h)
                        level(h, 4, 5)
                    if quarter == 1:
                        level(h, 5, 4, 4)
                    if quarter == 2:
                        level(h, 6, 5, 5)
                    if quarter == 3:
                        level(h, 7, 4, 6)

            with pe.Fori(0, H - 1) as h:
                head_first_half(h)
                for quarter in range(4):
                    group(0, quarter, 4 * h + 4, values_copied, h + 1)
                    if quarter == 0:
                        turn_keys(h)
                    if quarter == 1:
                        keys_values(h)
                    if quarter == 2:
                        spread(START_PIECES + h)
                    if quarter == 3:
                        outputs(h)
                for quarter in range(4):
                    group(1, quarter, 4 * h + 5, sig_used, 3 * h + 3)
                    if quarter == 1:
                        turn_outputs(h)
            last_head = H - 1
            head_first_half(last_head)
            turn_keys(last_head)
            keys_values(last_head)
            spread(PIECES - 1)
            pe.wait_ge(ada_rowed, PIECES)
            turn_mods(1)
            pe.wait_ge(mods_made, 3)
            outputs(last_head)

            def mix_out(i, u, q, first=False):
                pe.wait_ge(o_lo[q], i + 1)
                for kq in range(KD // 2):
                    k = q * (KD // 2) + kq
                    if first:
                        pe.wait_ge(wo_lo, k + 1)
                    for half in range(2):
                        for n, (a, b) in enumerate(PARTS):
                            last = pe.matmul(ps[:, 2 * u + half, :], o_split[:, q, a, kq, :],
                                             wo_split(k, b)[:, half * BANK:(half + 1) * BANK],
                                             start=(k == 0 and n == 0), stop=(k == KD - 1 and n == 2))
                last.then_inc(o_used[q], 1)

            def turn_x1(i):
                pe.wait_ge(x1_normed, i + 1)
                for k in range(KD):
                    last = turn(chunk(pair(2), k), chunk(norm_tile, k))
                last.then_inc(x1_turned, 1)

            mix_out(0, 0, 0, True)
            turn_outputs(last_head)
            mix_out(0, 0, 1, True)
            for q in range(2):
                mix_out(1, 1, q)
            turn_x1(0)
            with pe.Fori(0, NT // 2 - 1) as ii:
                for u in range(2):
                    i = 2 * ii + 2 + u
                    pe.wait_ge(x1_made, 2 * ii + u + 1)
                    for q in range(2):
                        mix_out(i, u, q)
                    turn_x1(i - 1)

            def up_half(s, half, done=None):
                for k in range(KD):
                    for n, (a, b) in enumerate(PARTS):
                        last = pe.matmul(ps[:, 2 * s + half, :], up_split[:, s, a, k, :],
                                         hT[:, b, k, half * BANK:(half + 1) * BANK],
                                         start=(k == 0 and n == 0), stop=(k == KD - 1 and n == 2))
                if done is not None:
                    last.then_inc(done, 1)

            pe.wait_ge(x1_made, NT - 1)
            pe.wait_ge(up_lo[0], 1)
            pe.wait_ge(h2_split, NT // 2)
            up_half(0, 0)
            pe.wait_ge(x1_made, NT)
            pe.wait_ge(up_lo[1], 1)
            up_half(1, 0)
            turn_x1(NT - 1)
            pe.wait_ge(h2_split, NT)
            up_half(0, 1, upped[0])
            up_half(1, 1, upped[1])
            with pe.Fori(1, FT) as j:
                for s in range(2):
                    pe.wait_ge(up_lo[s], j + 1)
                    pe.wait_ge(conved[s], j)
                    up_half(s, 0)
                    up_half(s, 1, upped[s])

            def down_tile(s, t, start, stop):
                for n, (a, b) in enumerate(PARTS):
                    last = pe.matmul(ps[:, t, :], a_split[:, s, a, t * P:(t + 1) * P], wd_split[:, s, b, :],
                                     start=(start and n == 0), stop=(stop and n == 2))
                return last

            def down_step(kk, s):
                pe.wait_ge(wd_lo, kk + 1)
                for t in range(NT):
                    last = down_tile(s, t, False, False)
                last.then_inc(downed, 1)

            def down_half(half):
                base = half * FT
                pe.wait_ge(wd_lo, base + 1)
                for t in range(NT):
                    if half == 1:
                        pe.wait_ge(left_kept, t + 1)
                    elif t in (0, 2):
                        pe.wait_ge(conved[t // 2], FT)
                    last = down_tile(0, t, True, False)
                last.then_inc(downed, 1)
                down_step(base + 1, 1)
                with pe.Fori(1, FT // 2 - 1) as kk:
                    for s in range(2):
                        down_step(base + 2 * kk + s, s)
                pe.wait_ge(wd_lo, base + FT)
                for t in range(NT):
                    last = down_tile(0, t, False, False)
                    if t == NT - 1:
                        last.then_inc(downed, 1)
                    down_tile(1, t, False, True).then_inc(y_bank, 1)

            down_half(0)
            down_half(1)


_INS = ["x", "c", "ada_w", "ada_b", "pre_mix_g", "post_mix_g", "pre_ffn_g", "post_ffn_g", "hgrn_w_in",
        "hgrn_lb_logits", "hgrn_gnorm_g", "hgrn_w_out", "ffn_w_up", "ffn_dw_w", "ffn_dw_b", "ffn_w_down"]


def kernel(**inputs):
    import numpy as _np
    import concourse.bacc as _bacc
    from concourse import mybir as _mybir
    from concourse.bass_utils import run_bass_kernel_spmd as _run

    nc = _bacc.Bacc("TRN2", target_bir_lowering=False, num_devices=1)
    arrays, args = {}, []
    for name in _INS:
        a = _np.ascontiguousarray(inputs[name])
        arrays[f"in_{name}"] = a
        args.append(nc.dram_tensor(f"in_{name}", a.shape, _mybir.dt.from_np(a.dtype), kind="ExternalInput").ap())
    shape = arrays["in_x"].shape
    args.append(nc.dram_tensor("out_x", shape, _mybir.dt.from_np(_np.dtype("float32")), kind="ExternalOutput").ap())
    hybrid_layer(nc, *args)
    r = _run(nc, [arrays], core_ids=[0])
    return r.results[0]["out_x"]
```

```python
from contextlib import ExitStack

import concourse.bass as bass
from concourse import mybir

ALU = mybir.AluOpType
ACT = mybir.ActivationFunctionType
F32 = mybir.dt.float32
F32R = mybir.dt.float32r
I32 = mybir.dt.int32
AX_X = mybir.AxisListType.X

P = 128
EPS = 1e-6
BANK = 512


class Tally:

    def __init__(self):
        self.base, self.n = 0, 0

    def up(self):
        self.n += 1
        return 1

    @property
    def now(self):
        return self.base + self.n

    def restart(self, base):
        self.base, self.n = base, 0


def hybrid_layer(nc, x, c, ada_w, ada_b, pre_mix_g, post_mix_g, pre_ffn_g, post_ffn_g,
                 w_in, lb_logits, gnorm_g, w_out, w_up, dw_w, dw_b, w_down, out):
    T, D = x.shape[1], x.shape[2]
    NT = T // P
    KD = D // P
    H = KD
    F = w_down.shape[1]
    FT = F // P
    TH = T // BANK
    LEVELS = 7
    MASKED = 5
    AC = BANK
    JH = KD // 2
    START_PIECES = 2 * D // AC
    PIECES = 6 * D // AC - START_PIECES
    CP = AC // P
    assert T == 1024 and D == 1024 and FT * P == F and NT == 8 and TH == 2 and PIECES == H

    x_rows = x.rearrange("b (n p) d -> (b n) p d", p=P)
    out_rows = out.rearrange("b (n p) d -> (b n) p d", p=P)
    ada_cols = ada_w.rearrange("l (j p) n -> p (l j) n", p=P)
    w_in_cols = w_in.rearrange("l (k p) n -> p (l k) n", p=P)
    w_out_rows = w_out.rearrange("l (k p) n -> (l k) p n", p=P)
    w_up_cols = w_up.rearrange("l (k p) n -> p (l k) n", p=P)
    w_down_rows = w_down.rearrange("l (k p) n -> (l k) p n", p=P)
    Q_COL, F_COL, I_COL, G_COL = 0, D, 2 * D, 3 * D
    x1_rows = nc.dram_tensor("x_after_mixer", (NT, P, D), F32, kind="Internal").ap()

    ctx = ExitStack()
    with ctx:
        def sb(name, shape, dt=F32, where=None):
            return (where or ctx).enter_context(nc.sbuf_tensor(name, shape, dt))

        def sem(name):
            return ctx.enter_context(nc.semaphore(name))

        ident = sb("ident", [P, P])
        ones = sb("ones", [P, P])
        level_mask = sb("level_mask", [P, MASKED, P // 2])
        minus_half = sb("minus_half", [P, 8])
        VR = 7 * KD + 1
        vec_cols = sb("vec_cols", [P, VR])
        dw_cols = sb("dw_cols", [P, 4, 2 * FT])
        mix_scale = sb("mix_scale", [P, KD])
        mix_shift = sb("mix_shift", [P, KD])
        ffn_scale = sb("ffn_scale", [P, KD])
        ffn_shift = sb("ffn_shift", [P, KD])
        low = sb("low", [P, H])
        high = sb("high", [P, H])
        cond = sb("cond", [P, KD])
        tiny = sb("tiny", [P, 8, 8])
        stat = sb("stat", [P, 8, 8])
        mod_rows = sb("mod_rows", [P, 4, D])
        mod_flat = mod_rows[:, :, :].rearrange("p v d -> p (v d)")

        early = ExitStack()
        hT = sb("hT", [P, 2, KD, T], F32R, early)

        mixer = ExitStack()
        oT = sb("oT", [P, H, T], F32, mixer)
        head = ExitStack()
        w_raw = sb("w_raw", [P, 2, KD, P], F32, head)
        ada_raw = sb("ada_raw", [P, 2, JH, AC], F32, head)
        w_split = sb("w_split", [P, 2, 2, KD, P], F32R, head)
        late = ExitStack()
        f_dec = sb("f_dec", [P, T], F32, late)
        gate = sb("gate", [P, T], F32, late)
        totals = sb("totals", [P, T], F32, late)
        k_dec = sb("k_dec", [P, T], F32, late)
        g_act = sb("g_act", [P, T], F32, late)
        v_tok = sb("v_tok", [P, NT, P], F32, late)
        scores = sb("scores", [P, T], F32, late)
        queries = sb("queries", [P, 2 * (T + 2)], F32, late)
        tok = sb("tok", [P, NT, P], F32, late)
        states = sb("states", [P, NT - 1, P], F32, late)
        ada_acc = sb("ada_acc", [P, AC], F32, late)
        ada_bias = sb("ada_bias", [1, AC], F32, late)
        late.close()
        q_act, q_dec = queries[:, 0:T], queries[:, T + 1:2 * T + 1]
        q_rows = queries[:, :].rearrange("p (g r) -> p g r", g=2)
        start = ExitStack()
        ada_more = sb("ada_more", [P, 3, JH, AC], F32, start)
        start.close()
        ada_slot = [ada_raw[:, 0], ada_raw[:, 1], ada_more[:, 0], ada_more[:, 1], ada_more[:, 2]]
        START_PE = 2
        ROW_BANK = [7, 7, 7, 3]
        START_COLS = [v * D + r * AC for r in range(2) for v in range(2)]
        start_acc = [ada_acc[:, :], states[:, 0:AC // P, :].rearrange("p n d -> p (n d)")]
        start_row = mod_flat[0:1, 0:AC]
        x_sb = oT
        vec_rows = tok[0:VR, 0, :]
        dw_rows = states[0:2 * FT, 0:4, :]
        h_f32 = [q_dec[:, 0:BANK], q_dec[:, BANK:T],
                 tok[:, 0:NT // 2, :].rearrange("p n d -> p (n d)"), tok[:, NT // 2:NT, :].rearrange("p n d -> p (n d)")]
        head.close()

        project = ExitStack()
        slabs = sb("slabs", [P, 3, D], F32, project)
        WO_EARLY = 5
        wo_early = sb("wo_early", [P, WO_EARLY, 2, D], F32R, project)
        o_split = sb("o_split", [P, 2, 2, KD // 2, P], F32R, project)
        wo_late = sb("wo_late", [P, KD - WO_EARLY, 2, D], F32R, project)
        norm_tile = slabs[:, 0, :]

        def wo_split(k, part):
            return wo_early[:, k, part, :] if k < WO_EARLY else wo_late[:, k - WO_EARLY, part, :]

        project.close()
        mixer.close()

        up = ExitStack()
        raw = ExitStack()
        up_raw = sb("up_raw", [P, 2, KD, P], F32, raw)
        raw.close()
        wd_split0 = sb("wd_split0", [P, 2, BANK], F32R, up)
        wd_raw01 = sb("wd_raw01", [P, 2, BANK], F32, up)
        up_split = sb("up_split", [P, 2, 2, KD, P], F32R, up)
        act = sb("act", [P, FT, T], F32, up)
        a_split0 = sb("a_split0", [P, 2, T], F32R, up)
        conv_a, conv_b, sig_a = mod_rows[:, 0, :], mod_rows[:, 1, :], mod_rows[:, 2, :]
        up.close()
        early.close()

        down = ExitStack()
        a_split1 = sb("a_split1", [P, 2, T], F32R, down)
        wd_split1 = sb("wd_split1", [P, 2, BANK], F32R, down)
        a_split2 = sb("a_split2", [P, 2, T], F32R, down)
        wd_split2 = sb("wd_split2", [P, 2, BANK], F32R, down)
        wd_raw23 = sb("wd_raw23", [P, 2, BANK], F32, down)
        y_gained = sb("y_gained", [P, NT, D], F32, down)
        down.close()
        a_split = [a_split0, a_split1, a_split2]
        wd_split = [wd_split0, wd_split1, wd_split2]
        wd_raw = [wd_raw01[:, 0, :], wd_raw01[:, 1, :], wd_raw23[:, 0, :], wd_raw23[:, 1, :]]
        out_sb = act[:, 0:NT, :]
        POOL_TILES = (1, 4)
        squares = act[:, NT:NT + NT // 2, :].rearrange("p n (two d) -> p (n two) d", two=2)

        ps = ctx.enter_context(nc.psum_tensor("ps", [P, 8, BANK], F32))

        def pair(n):
            return ps[:, 2 * n:2 * n + 2, :].rearrange("p a b -> p (a b)")

        UNITS = [(r * (KD // 2) + n, half) for r in range(2) for half in range(2) for n in range(KD // 2)]
        UNIT_BANK = [4, 5, 6, 2, 3] + [4 + u % 3 for u in range(NT + KD - 5)]
        UNIT_BEFORE = [max([v for v in range(u) if UNIT_BANK[v] == UNIT_BANK[u]], default=None)
                       for u in range(NT + KD)]

        TAKES = LEVELS + 2

        def masks(n):
            return 2 * n if n <= 2 else n + 2

        vec_in = sem("vec_in")
        dw_in = sem("dw_in")
        x_in = [sem(f"x_in{i}") for i in range(NT)]
        w_in_arrived = [sem(f"w_in_arrived{s}") for s in range(2)]
        start_in = [sem(f"start_in{m}") for m in range(2 * START_PIECES)]
        ada_in = [sem(f"ada_in{s}") for s in range(2)]
        post_in = sem("post_in")
        wo_in = [sem(f"wo_in{s}") for s in range(2)]
        xt_in = [sem(f"xt_in{u}") for u in range(2)]
        x1_stored = [sem(f"x1_stored{u}") for u in range(2)]
        up_in = [sem(f"up_in{s}") for s in range(2)]
        wd_in = [sem(f"wd_in{s}") for s in range(4)]
        x1_back = [sem(f"x1_back{t}") for t in range(NT)]
        out_stored = sem("out_stored")

        pool_own = sem("pool_own")
        consts_made = sem("consts_made")
        rooted = sem("rooted")

        dve_own = sem("dve_own")
        vecs_turned = sem("vecs_turned")
        dw_turned = sem("dw_turned")
        vecs_copied = sem("vecs_copied")
        lb_shifted = sem("lb_shifted")
        lb_exp = sem("lb_exp")
        c_sig = sem("c_sig")
        x_squared = sem("x_squared")
        x_mean = sem("x_mean")
        x_normed = sem("x_normed")
        x_turned = sem("x_turned")
        h_scaled = sem("h_scaled")
        h_split = sem("h_split")
        cond_made = sem("cond_made")
        start_summed = sem("start_summed")
        start_rowed = sem("start_rowed")
        start_copied = sem("start_copied")
        start_turned = sem("start_turned")
        mix_made = sem("mix_made")
        ada_used = sem("ada_used")
        ada_summed = sem("ada_summed")
        ada_spread = sem("ada_spread")
        ada_rowed = sem("ada_rowed")
        mod_turned = sem("mod_turned")
        mods_made = sem("mods_made")

        w_hi = sem("w_hi")
        w_lo = sem("w_lo")
        projected = sem("projected")
        sig_done = sem("sig_done")
        sig_used = sem("sig_used")
        values_copied = sem("values_copied")
        values_turned = sem("values_turned")
        v_ready = sem("v_ready")
        decayed = sem("decayed")
        scored = sem("scored")
        masked = sem("masked")
        keys_turned = sem("keys_turned")
        keys_ready = sem("keys_ready")
        chunk_kv = sem("chunk_kv")
        states_ready = sem("states_ready")
        o_ready = sem("o_ready")
        o_squared = sem("o_squared")
        o_mean = sem("o_mean")
        o_normed = sem("o_normed")
        o_turned = sem("o_turned")
        head_out = sem("head_out")

        wo_hi = sem("wo_hi")
        wo_lo = sem("wo_lo")
        o_hi = [sem(f"o_hi{q}") for q in range(2)]
        o_lo = [sem(f"o_lo{q}") for q in range(2)]
        o_used = [sem(f"o_used{q}") for q in range(2)]
        y_squared = sem("y_squared")
        y_mean = sem("y_mean")
        x1_made = sem("x1_made")
        x1_squared = sem("x1_squared")
        x1_mean = sem("x1_mean")
        x1_normed = sem("x1_normed")
        x1_turned = sem("x1_turned")
        h2_scaled = sem("h2_scaled")
        h2_split = sem("h2_split")

        up_hi = [sem(f"up_hi{s}") for s in range(2)]
        up_lo = [sem(f"up_lo{s}") for s in range(2)]
        upped = [sem(f"upped{s}") for s in range(2)]
        tap0 = [sem(f"tap0{s}") for s in range(2)]
        conved = [sem(f"conved{s}") for s in range(2)]
        a_sig = sem("a_sig")
        gated = sem("gated")

        a_hi = sem("a_hi")
        a_lo = sem("a_lo")
        wd_hi = sem("wd_hi")
        wd_lo = sem("wd_lo")
        downed = sem("downed")
        y_bank = sem("y_bank")
        out_squared = sem("out_squared")
        left_kept = sem("left_kept")
        right_kept = sem("right_kept")
        left_mean = sem("left_mean")
        out_mean = sem("out_mean")
        out_rooted = sem("out_rooted")
        out_made = sem("out_made")
        out_scaled = sem("out_scaled")
        pool_made = sem("pool_made")

        block = ctx.enter_context(nc.Block())

        @block.sync
        def _(sp):
            for i, rows in enumerate((c, pre_mix_g, pre_ffn_g)):
                sp.dma_start(vec_rows[i * KD:(i + 1) * KD, :],
                             rows.rearrange("a (k p) -> (a k) p", p=P)).then_inc(vec_in, 16)
            sp.dma_start(vec_rows[3 * KD:5 * KD, :],
                         lb_logits.rearrange("a (k p) -> (a k) p", p=P)).then_inc(vec_in, 16)
            sp.dma_start(vec_rows[5 * KD:7 * KD, :],
                         ada_b[:, 0:2 * D].rearrange("a (k p) -> (a k) p", p=P)).then_inc(vec_in, 16)
            sp.dma_start(vec_rows[7 * KD:VR, :], gnorm_g).then_inc(vec_in, 16)
            sp.dma_start(dw_rows[:, 0:3, :], dw_w.rearrange("a t (n p) -> n (a t) p", p=P)).then_inc(dw_in, 16)
            sp.dma_start(dw_rows[:, 3, :], dw_b.rearrange("a (n p) -> (a n) p", p=P)).then_inc(dw_in, 16)

            def load_w(n, col):
                sp.dma_start(w_raw[:, n % 2, :, :], w_in_cols[:, :, col]).then_inc(w_in_arrived[n % 2], 16)

            def load_piece(p):
                for s in range(2):
                    if not isinstance(p, int) or p > 0:
                        sp.wait_ge(ada_used, 2 * p - 1 + s)
                    sp.dma_start(ada_raw[:, s, :, :], ada_cols[:, s * JH:(s + 1) * JH,
                                                               bass.ts(p + START_PIECES, AC)]).then_inc(ada_in[s], 16)
                    if s == 1:
                        if not isinstance(p, int) or p > 0:
                            sp.wait_ge(ada_summed, p)
                        sp.dma_start(ada_bias[:, :], ada_b[:, bass.ts(p + START_PIECES, AC)]).then_inc(ada_in[1], 16)

            for i in range(NT):
                sp.dma_start(x_sb[:, i, :], x_rows[i]).then_inc(x_in[i], 16)
            for m in range(2 * START_PIECES):
                before = m - len(ada_slot)
                if before >= 0:
                    sp.wait_ge((start_summed, start_rowed)[before % 2], before // 2 + 1)
                col, k = START_COLS[m // 2], m % 2 * JH
                sp.dma_start(ada_slot[m % len(ada_slot)],
                             ada_cols[:, k:k + JH, col:col + AC]).then_inc(start_in[m], 16)
                if m == 3:
                    load_w(0, slice(F_COL, F_COL + P))
                if m == 5:
                    load_w(1, slice(Q_COL, Q_COL + P))
            sp.wait_ge(w_lo, 1)
            load_w(2, slice(I_COL, I_COL + P))
            sp.wait_ge(w_lo, 2)
            load_w(3, slice(G_COL, G_COL + P))
            sp.wait_ge(start_rowed, START_PIECES)
            load_piece(0)
            with sp.Fori(0, H - 1) as h:
                sp.wait_ge(w_lo, 4 * h + 3)
                load_w(0, bass.ds(F_COL + P + h * P, P))
                sp.wait_ge(w_lo, 4 * h + 4)
                load_w(1, bass.ds(Q_COL + P + h * P, P))
                sp.wait_ge(w_lo, 4 * h + 5)
                load_w(0, bass.ds(I_COL + P + h * P, P))
                load_piece(h + 1)
                sp.wait_ge(w_lo, 4 * h + 6)
                load_w(1, bass.ds(G_COL + P + h * P, P))

            sp.wait_ge(w_lo, 4 * H)
            sp.wait_ge(ada_summed, PIECES)
            for k in range(KD):
                if k >= 2:
                    sp.wait_ge(wo_lo, k - 1)
                sp.dma_start(slabs[:, 1 + k % 2, :], w_out_rows[k]).then_inc(wo_in[k % 2], 16)
                if k == 1:
                    sp.dma_start(slabs[:, 0, :], post_mix_g.broadcast_to((P, D))).then_inc(post_in, 16)
                if k == 3:
                    sp.wait_ge(mods_made, 1)
                    sp.dma_start(slabs[:, 0, :], post_ffn_g.broadcast_to((P, D))).then_inc(post_in, 16)
            sp.wait_ge(wo_lo, KD)
            sp.dma_start(slabs[:, 1, :], x_rows[0]).then_inc(xt_in[0], 16)
            sp.dma_start(slabs[:, 2, :], x_rows[1]).then_inc(xt_in[1], 16)
            with sp.Fori(0, NT // 2 - 1) as ii:
                for u in range(2):
                    sp.wait_ge(x1_made, 2 * ii + u + 1)
                    sp.dma_start(x1_rows[2 * ii + u], mod_rows[:, 1 + u, :]).then_inc(x1_stored[u], 16)
                    sp.dma_start(slabs[:, 1 + u, :], x_rows[2 * ii + u + 2]).then_inc(xt_in[u], 16)
            sp.wait_ge(o_lo[1], NT)
            sp.dma_start(up_raw[:, 0, :, :], w_up_cols[:, :, 0:P]).then_inc(up_in[0], 16)
            sp.dma_start(up_raw[:, 1, :, :], w_up_cols[:, :, F:F + P]).then_inc(up_in[1], 16)
            for u in range(2):
                sp.wait_ge(x1_made, NT - 1 + u)
                sp.dma_start(x1_rows[NT - 2 + u], mod_rows[:, 1 + u, :]).then_inc(x1_stored[u], 16)
            with sp.Fori(0, FT - 1) as j:
                for s in range(2):
                    sp.wait_ge(up_lo[s], j + 1)
                    sp.dma_start(up_raw[:, s, :, :],
                                 w_up_cols[:, :, bass.ds(s * F + P + j * P, P)]).then_inc(up_in[s], 16)

            for kk in range(4):
                if kk == 0:
                    sp.wait_ge(up_lo[1], FT)
                if kk == 2:
                    sp.wait_ge(upped[1], FT)
                sp.dma_start(wd_raw[kk], w_down_rows[kk, :, 0:BANK]).then_inc(wd_in[kk], 16)
            with sp.Fori(1, FT // 4) as m:
                for s in range(4):
                    sp.wait_ge(wd_lo, 4 * m + s - 3)
                    sp.dma_start(wd_raw[s], w_down_rows[4 * m + s, :, 0:BANK]).then_inc(wd_in[s], 16)
            for s in range(2):
                sp.wait_ge(wd_lo, FT + s - 5)
                sp.dma_start(wd_raw[s], w_down_rows[FT - 2 + s, :, 0:BANK]).then_inc(wd_in[s], 16)
            for s in range(2):
                sp.wait_ge(wd_lo, FT + s - 3)
                sp.dma_start(wd_raw[2 + s], w_down_rows[s, :, BANK:D]).then_inc(wd_in[2 + s], 16)
            def load_right(m, s):
                sp.wait_ge(wd_lo, FT + 4 * m + s - 1)
                sp.dma_start(wd_raw[s], w_down_rows[4 * m + s + 2, :, BANK:D]).then_inc(wd_in[s], 16)

            with sp.Fori(0, FT // 4 - 2) as m:
                for s in range(4):
                    load_right(m, s)
            for u in range(2):
                sp.wait_ge(x1_stored[u], 16 * NT // 2)
            for m in range(2):
                for s in range(4):
                    load_right(FT // 4 - 2 + m, s)
                    t = 4 * m + s
                    sp.wait_ge(a_lo, FT + t + 1)
                    sp.dma_start(out_sb[:, t, :], x1_rows[t]).then_inc(x1_back[t], 16)
            for t in (0, 2, 1, 3, 5, 4, 6, 7):
                if t in POOL_TILES:
                    sp.wait_ge(pool_made, POOL_TILES.index(t) + 1)
                else:
                    sp.wait_ge(out_made, t + 1 - len([n for n in POOL_TILES if n < t]))
                sp.dma_start(out_rows[t], out_sb[:, t, :]).then_inc(out_stored, 16)
            sp.wait_ge(out_stored, 16 * NT)

        @block.gpsimd
        def _(pool):
            own = Tally()
            pool.memset(ident[:, :], 0.0).then_inc(pool_own, own.up())
            pool.memset(level_mask[:, :, :], 1.0).then_inc(pool_own, own.up())
            pool.memset(ones[:, :], 1.0).then_inc(consts_made, 1)
            pool.memset(minus_half[:, :], -0.5).then_inc(consts_made, 1)
            pool.wait_ge(pool_own, own.now)
            pool.affine_select(out=ident[:, :], in_=ident[:, :], compare_op=ALU.not_equal, fill=1.0, base=0,
                               pattern=[[-1, P]], channel_multiplier=1).then_inc(consts_made, 1)
            for j in range(MASKED):
                half = 1 << j
                m = level_mask[:, j, :].rearrange("p (n w) -> p n w", w=half)
                blocks = P // (2 * half)
                pool.affine_select(out=m, in_=m, compare_op=ALU.is_ge, fill=0.0, base=0,
                                   pattern=[[-2 * half, blocks], [0, half]],
                                   channel_multiplier=1).then_inc(pool_own, own.up())
                pool.wait_ge(pool_own, own.now)
                pool.affine_select(out=m, in_=m, compare_op=ALU.is_ge, fill=0.0, base=half - 1,
                                   pattern=[[2 * half, blocks], [0, half]],
                                   channel_multiplier=-1).then_inc(consts_made, 1)
            pool.memset(scores[:, :], 0.0).then_inc(consts_made, 1)
            pool.wait_ge(consts_made, 2)
            for r in range(2):
                some = slice(r * (NT // 2), (r + 1) * (NT // 2))
                pool.wait_ge(x_mean, r + 1)
                pool.tensor_tensor(stat[:, 0, some], tiny[:, 0, some], minus_half[:, 0:NT // 2],
                                   ALU.pow).then_inc(rooted, 1)
            with pool.Fori(0, H) as h:
                pool.wait_ge(o_mean, h + 1)
                pool.tensor_tensor(stat[:, 1, :], tiny[:, 1, :], minus_half[:, :], ALU.pow).then_inc(rooted, 1)
            with pool.Fori(0, NT) as i:
                pool.wait_ge(y_mean, i + 1)
                pool.tensor_tensor(stat[:, 2, 0:1], tiny[:, 2, 0:1], minus_half[:, 0:1],
                                   ALU.pow).then_inc(rooted, 1)
                pool.wait_ge(x1_mean, i + 1)
                pool.tensor_tensor(stat[:, 3, 0:1], tiny[:, 3, 0:1], minus_half[:, 0:1],
                                   ALU.pow).then_inc(rooted, 1)
            for t in range(NT):
                pool.wait_ge(out_mean, t + 1)
                pool.tensor_tensor(stat[:, 4, t:t + 1], tiny[:, 4, t:t + 1], minus_half[:, 0:1],
                                   ALU.pow).then_inc(out_rooted, 1)
                if t - 2 in POOL_TILES:
                    pool.wait_ge(out_scaled, POOL_TILES.index(t - 2) + 1)
                    pool.wait_ge(x1_back[t - 2], 16)
                    pool.tensor_tensor(out_sb[:, t - 2, :], y_gained[:, t - 2, :], out_sb[:, t - 2, :],
                                       ALU.add).then_inc(pool_made, 1)

        @block.scalar
        def _(sa):
            for i in range(NT):
                sa.wait_ge(x_in[i], 16)
                if i > 0:
                    sa.wait_ge(x_squared, i)
                sa.activation(pair(0), x_sb[:, i, :], ACT.Square,
                              accum_out=tiny[:, 5, i:i + 1]).then_inc(x_squared, 1)
                if i == 1:
                    sa.wait_ge(lb_shifted, 1)
                    sa.activation(stat[:, 5:7, :], stat[:, 5:7, :], ACT.Exp).then_inc(lb_exp, 1)
                    sa.activation(cond[:, :], vec_cols[:, 0:KD], ACT.Sigmoid).then_inc(c_sig, 1)

            def split_w(n, s, load):
                sa.wait_ge(w_in_arrived[s], 16 * load)
                if not isinstance(n, int) or n >= 2:
                    sa.wait_ge(projected, n - 1)
                sa.activation(w_split[:, s, 0, :, :], w_raw[:, s, :, :], ACT.Copy).then_inc(w_hi, 1)

            def ada_row(p, dst):
                sa.wait_ge(ada_spread, p + 1)
                sa.activation(mod_flat[:, bass.ts(dst, AC)], ps[:, 6, :], ACT.Copy).then_inc(ada_rowed, 1)

            def copy_start(p):
                sa.wait_ge(start_rowed, p + 1)
                sa.activation(start_row, ps[0:1, ROW_BANK[p], :], ACT.Copy).then_inc(start_copied, 1)

            copy_start(0)
            split_w(0, 0, 1)
            copy_start(1)
            for u, (k, half) in enumerate(UNITS):
                if u % NT == 0:
                    sa.wait_ge(mix_made, 2 * (u // NT) + 2)
                sa.wait_ge(x_turned, u + 1)
                if u >= 4:
                    sa.wait_ge(h_split, u - 3)
                for dst in (h_f32[u % 4], hT[:, 0, k, 0:BANK])[:2 - half]:
                    last = sa.activation(dst, ps[:, UNIT_BANK[u], :], ACT.Identity, bias=mix_shift[:, k:k + 1],
                                         scale=mix_scale[:, k:k + 1])
                last.then_inc(h_scaled, 1)
                if u == 3:
                    split_w(1, 1, 1)
                    copy_start(2)
                if u == NT - 1:
                    copy_start(3)

            def sigmoid_f(h):
                sa.wait_ge(projected, 4 * h + 1)
                if not isinstance(h, int) or h > 0:
                    sa.wait_ge(sig_used, 3 * h)
                sa.activation(gate[:, :], pair(0), ACT.Sigmoid).then_inc(sig_done, 1)

            def head_front(h):
                sa.wait_ge(projected, 4 * h + 2)
                sa.wait_ge(sig_used, 3 * h + 1)
                sa.activation(gate[:, :], pair(1), ACT.Sigmoid).then_inc(sig_done, 1)
                split_w(4 * h + 3, 1, 2 * h + 2)
                sa.wait_ge(projected, 4 * h + 3)
                sa.wait_ge(sig_used, 3 * h + 2)
                sa.activation(gate[:, :], pair(0), ACT.Copy).then_inc(values_copied, 1)

            def head_values(h):
                sa.wait_ge(values_turned, h + 1)
                sa.activation(v_tok[:, :, :].rearrange("p n d -> p (n d)"), pair(3), ACT.Copy).then_inc(v_ready, 1)

            def sigmoid_g(h):
                sa.wait_ge(projected, 4 * h + 4)
                sa.activation(gate[:, :], pair(1), ACT.Sigmoid).then_inc(sig_done, 1)

            def head_keys(h):
                sa.wait_ge(keys_turned, h + 1)
                sa.activation(tok[:, :, :].rearrange("p n d -> p (n d)"), pair(3), ACT.Copy).then_inc(keys_ready, 1)

            def head_square(h):
                sa.wait_ge(o_ready, h + 1)
                sa.activation(tok[:, :, :].rearrange("p n d -> p (n d)"), pair(3), ACT.Square).then_inc(o_squared, 1)

            sigmoid_f(0)
            split_w(2, 0, 2)
            with sa.Fori(0, H - 1) as h:
                head_front(h)
                split_w(4 * h + 4, 0, 2 * h + 3)
                head_values(h)
                sigmoid_g(h)
                split_w(4 * h + 5, 1, 2 * h + 3)
                head_keys(h)
                ada_row(h, h)
                sigmoid_f(h + 1)
                head_square(h)
                split_w(4 * h + 6, 0, 2 * h + 4)

            def split_wo(k):
                sa.wait_ge(wo_in[k % 2], 16 * (k // 2 + 1))
                sa.activation(wo_split(k, 0), slabs[:, 1 + k % 2, :], ACT.Copy).then_inc(wo_hi, 1)

            def split_o(i, q):
                if not isinstance(i, int) or i > 0:
                    sa.wait_ge(o_used[q], i)
                sa.activation(o_split[:, q, 0, :, :],
                              oT[:, q * (KD // 2):(q + 1) * (KD // 2), bass.ts(i, P)],
                              ACT.Copy).then_inc(o_hi[q], 1)

            head_front(H - 1)
            split_wo(0)
            head_values(H - 1)
            split_wo(1)
            sigmoid_g(H - 1)
            split_wo(2)
            ada_row(PIECES - 1, PIECES - 1)
            head_keys(H - 1)
            split_o(0, 0)
            split_wo(3)
            sa.wait_ge(sig_used, 3 * H)
            sa.wait_ge(states_ready, H)
            split_wo(4)
            head_square(H - 1)

            def square_y(i, u):
                sa.wait_ge(o_used[1], i + 1)
                sa.activation(pair(3), pair(u), ACT.Square, accum_out=tiny[:, 6, 0:1]).then_inc(y_squared, 1)

            def scale_h2(i, ks=range(KD)):
                sa.wait_ge(x1_turned, i + 1)
                for k in ks:
                    done = sa.activation(norm_tile[:, k * P:(k + 1) * P], pair(2)[:, k * P:(k + 1) * P],
                                         ACT.Identity, bias=ffn_shift[:, k:k + 1], scale=ffn_scale[:, k:k + 1])
                done.then_inc(h2_scaled, 1)

            def norm_x1(i, u):
                sa.wait_ge(x1_made, i + 1)
                sa.activation(pair(3), mod_rows[:, 1 + u, :], ACT.Square,
                              accum_out=tiny[:, 7, 0:1]).then_inc(x1_squared, 1)
                if not isinstance(i, int) or i > 0:
                    sa.wait_ge(h2_split, i)
                sa.wait_ge(rooted, 2 + H + 2 * i + 2)
                sa.activation(norm_tile, mod_rows[:, 1 + u, :], ACT.Copy,
                              scale=stat[:, 3, 0:1]).then_inc(x1_normed, 1)

            split_wo(5)
            split_o(1, 0)
            sa.wait_ge(o_turned, H)
            split_wo(6)
            sa.wait_ge(head_out, H)
            split_o(0, 1)
            split_wo(7)
            sa.wait_ge(mods_made, 3)
            split_o(1, 1)
            square_y(0, 0)
            norm_x1(0, 0)

            def mixer_tile(i, u):
                split_o(i + 1, 0)
                square_y(i, u)
                split_o(i + 1, 1)
                scale_h2(i - 1)
                norm_x1(i, u)

            mixer_tile(1, 1)
            with sa.Fori(1, NT // 2 - 1) as ii:
                for u in range(2):
                    mixer_tile(2 * ii + u, u)
            mixer_tile(NT - 2, 0)

            def split_up(j, s):
                sa.wait_ge(up_in[s], 16 * (j + 1))
                if not isinstance(j, int) or j > 0:
                    sa.wait_ge(upped[s], j)
                sa.activation(up_split[:, s, 0, :, :], up_raw[:, s, :, :], ACT.Copy).then_inc(up_hi[s], 1)

            sa.wait_ge(o_lo[1], NT)
            split_up(0, 0)
            split_up(0, 1)
            square_y(NT - 1, 1)
            scale_h2(NT - 2)
            norm_x1(NT - 1, 1)
            scale_h2(NT - 1, range(0, KD // 2))
            scale_h2(NT - 1, range(KD // 2, KD))

            def first_tap(j, s, dst):
                ft = j + s * FT
                sa.wait_ge(upped[s], j + 1)
                if not isinstance(j, int) or j > 0:
                    sa.wait_ge(gated, j)
                sa.activation(dst, pair(s), ACT.Identity, bias=dw_cols[:, 3, bass.ds(ft, 1)],
                              scale=dw_cols[:, 2, bass.ds(ft, 1)]).then_inc(tap0[s], 1)

            def sigmoid_a(j):
                sa.wait_ge(conved[0], j + 1)
                sa.activation(sig_a, conv_a, ACT.Sigmoid).then_inc(a_sig, 1)

            for u in range(2):
                sa.wait_ge(x1_stored[u], 16 * NT // 2)
            first_tap(0, 0, conv_a)
            split_up(1, 0)
            sigmoid_a(0)
            first_tap(0, 1, conv_b)
            split_up(1, 1)
            with sa.Fori(1, FT - 1) as j:
                first_tap(j, 0, conv_a)
                split_up(j + 1, 0)
                sigmoid_a(j)
                first_tap(j, 1, conv_b)
                split_up(j + 1, 1)
            first_tap(FT - 1, 0, conv_a)
            sigmoid_a(FT - 1)

            def split_down(kk, k, r, load, freed=lambda kk: kk - 1, s=None):
                s = r % 2 if s is None else s
                if freed:
                    sa.wait_ge(downed, freed(kk))
                sa.activation(a_split[s][:, 0, :], act[:, k, :], ACT.Copy).then_inc(a_hi, 1)
                sa.wait_ge(wd_in[r], 16 * load)
                sa.activation(wd_split[s][:, 0, :], wd_raw[r], ACT.Copy).then_inc(wd_hi, 1)

            def square_out(half, t):
                sa.wait_ge(y_bank, half * NT + t + 1)
                sa.activation(y_gained[:, t, 0:BANK] if half == 0 else squares[:, t, :], ps[:, t, :], ACT.Square,
                              accum_out=tiny[:, half, t:t + 1]).then_inc(out_squared, 1)

            sa.wait_ge(up_lo[1], FT)
            split_down(0, 0, 0, 1, None)
            first_tap(FT - 1, 1, conv_b)
            split_down(1, 1, 1, 1, None)
            split_down(2, 2, 2, 1)
            split_down(3, 3, 3, 1)
            with sa.Fori(1, FT // 4) as m:
                for r in range(4):
                    split_down(4 * m + r, 4 * m + r, r, m + 1)
            sa.wait_ge(gated, FT)
            split_down(FT - 2, FT - 2, 0, FT // 4 + 1)
            split_down(FT - 1, FT - 1, 1, FT // 4 + 1)
            split_down(FT, 0, 2, FT // 4 + 1)
            for t in range(NT):
                square_out(0, t)
            split_down(FT + 1, 1, 3, FT // 4 + 1, None)
            with sa.Fori(0, FT // 4 - 1) as m:
                for r in range(4):
                    split_down(FT + 2 + 4 * m + r, 4 * m + r + 2, r, m + (FT // 4 + 2),
                               lambda kk: kk - 2)
            for r in range(3):
                split_down(2 * FT - 4 + r, FT - 4 + r, r, 2 * (FT // 4) + 1, lambda kk: kk - 2)
            split_down(2 * FT - 1, FT - 1, 3, 2 * (FT // 4) + 1, None, 2)
            for t in range(NT):
                square_out(1, t)
                if t - 2 in POOL_TILES:
                    sa.wait_ge(right_kept, t - 1)
                    sa.wait_ge(out_rooted, t - 1)
                    sa.activation(y_gained[:, t - 2, :], y_gained[:, t - 2, :], ACT.Copy,
                                  scale=stat[:, 4, t - 2:t - 1]).then_inc(out_scaled, 1)

        @block.vector
        def _(ve):
            own = Tally()

            def link(ins):
                ins.then_inc(dve_own, own.up())
                ve.wait_ge(dve_own, own.now)

            ve.wait_ge(vecs_turned, 1)
            ve.tensor_copy(vec_cols[:, :], ps[:, 4, 0:VR]).then_inc(vecs_copied, 1)
            ve.wait_ge(vecs_copied, 1)
            l0, l1 = vec_cols[:, 3 * KD:4 * KD], vec_cols[:, 4 * KD:5 * KD]
            e0, e1 = stat[:, 5, :], stat[:, 6, :]
            link(ve.tensor_tensor(stat[:, 7, :], l0, l1, ALU.max))
            ve.tensor_tensor(e0, l0, stat[:, 7, :], ALU.subtract)
            ve.tensor_tensor(e1, l1, stat[:, 7, :], ALU.subtract).then_inc(lb_shifted, 1)
            ve.wait_ge(dw_turned, 1)
            ve.tensor_copy(dw_cols[:, :, :].rearrange("p t n -> p (t n)"), ps[:, 5, 0:8 * FT]).then_inc(vecs_copied, 1)
            ve.wait_ge(lb_exp, 1)
            link(ve.tensor_tensor(stat[:, 7, :], e0, e1, ALU.add))
            link(ve.reciprocal(stat[:, 7, :], stat[:, 7, :]))
            link(ve.tensor_tensor(low[:, :], e0, stat[:, 7, :], ALU.mult))
            ve.tensor_scalar(high[:, :], low[:, :], -1.0, 1.0, ALU.mult, ALU.add)
            ve.wait_ge(c_sig, 1)
            ve.tensor_tensor(cond[:, :], cond[:, :], vec_cols[:, 0:KD], ALU.mult).then_inc(cond_made, 1)
            ve.wait_ge(cond_made, 1)

            for r in range(2):
                some = slice(r * (NT // 2), (r + 1) * (NT // 2))
                ve.wait_ge(x_squared, (r + 1) * (NT // 2))
                ve.tensor_scalar(tiny[:, 0, some], tiny[:, 5, some], 1.0 / D, EPS,
                                 ALU.mult, ALU.add).then_inc(x_mean, 1)
                ve.wait_ge(rooted, r + 1)
                for i in range(r * (NT // 2), (r + 1) * (NT // 2)):
                    ve.tensor_scalar(x_sb[:, i, :], x_sb[:, i, :], stat[:, 0, i:i + 1], None,
                                     ALU.mult).then_inc(x_normed, 1)

            def split_w(n, s):
                ve.wait_ge(w_hi, n + 1)
                ve.tensor_tensor(w_split[:, s, 1, :, :], w_raw[:, s, :, :], w_split[:, s, 0, :, :].bitcast(F32),
                                 ALU.subtract).then_inc(w_lo, 1)

            def ada_quarter(p, c):
                acc = ada_acc[:, :]
                s = c // 2
                if c % 2 == 0:
                    ve.wait_ge(ada_in[s], 16 * (s + 1) * (p + 1))
                for k in (2 * c, 2 * c + 1):
                    j = k % JH
                    if k == 0:
                        ins = ve.tensor_scalar(acc, ada_raw[:, s, j, :], cond[:, k:k + 1], None, ALU.mult)
                    else:
                        ins = ve.scalar_tensor_tensor(out=acc, in0=ada_raw[:, s, j, :], scalar=cond[:, k:k + 1],
                                                      in1=acc, op0=ALU.mult, op1=ALU.add)
                    if j == JH - 1:
                        ins.then_inc(ada_used, 1)
                        ve.wait_ge(ada_used, 2 * p + s + 1)
                    else:
                        link(ins)
                if c == 3:
                    ve.tensor_tensor(ada_acc[0:1, :], ada_acc[0:1, :], ada_bias[:, :], ALU.add).then_inc(ada_summed, 1)

            def start_piece(p):
                acc = start_acc[p % 2]
                ve.wait_ge(start_in[2 * p], 16)
                if p >= 2:
                    ve.wait_ge(start_rowed, p - 1)
                for j in range(KD - START_PE):
                    m = 2 * p + j // JH
                    if j == JH:
                        ve.wait_ge(start_in[m], 16)
                    src = ada_slot[m % len(ada_slot)][:, j % JH, :]
                    if j == 0:
                        ins = ve.tensor_scalar(acc, src, cond[:, j:j + 1], None, ALU.mult)
                    else:
                        ins = ve.scalar_tensor_tensor(out=acc, in0=src, scalar=cond[:, j:j + 1],
                                                      in1=acc, op0=ALU.mult, op1=ALU.add)
                    if j < KD - START_PE - 1:
                        link(ins)
                ins.then_inc(start_summed, 1)

            def start_mod(p):
                some = slice(p // 2 * CP, (p // 2 + 1) * CP)
                first = 5 * KD + p % 2 * KD + p // 2 * CP
                bias = vec_cols[:, first:first + CP]
                ve.wait_ge(start_turned, p + 1)
                if p % 2 == 0:
                    ve.tensor_tensor(mix_shift[:, some], ps[:, ROW_BANK[p], 0:CP], bias, ALU.add).then_inc(mix_made, 1)
                else:
                    link(ve.scalar_tensor_tensor(out=mix_scale[:, some], in0=ps[:, ROW_BANK[p], 0:CP], scalar=1.0, in1=bias,
                                                 op0=ALU.add, op1=ALU.add))
                    ve.tensor_tensor(mix_scale[:, some], mix_scale[:, some],
                                     vec_cols[:, KD:2 * KD][:, some], ALU.mult).then_inc(mix_made, 1)

            def modulation(shift, scale, gain):
                ve.tensor_copy(shift[:, :], ps[:, 1, 0:KD])
                return ve.scalar_tensor_tensor(out=scale[:, :], in0=ps[:, 1, KD:2 * KD], scalar=1.0, in1=gain,
                                               op0=ALU.add, op1=ALU.mult)

            def split_units(first, end):
                for u in range(first, end):
                    k, half = UNITS[u]
                    hi, lo = (hT[:, part, k, half * BANK:(half + 1) * BANK] for part in range(2))
                    ve.wait_ge(h_scaled, u + 1)
                    if half == 1:
                        link(ve.tensor_copy(hi, h_f32[u % 4]))
                    ve.tensor_tensor(lo, h_f32[u % 4], hi.bitcast(F32), ALU.subtract).then_inc(h_split, 1)

            start_piece(0)
            start_piece(1)
            start_mod(0)
            split_w(0, 0)
            start_mod(1)
            start_piece(2)
            split_units(0, 4)
            split_w(1, 1)
            start_piece(3)
            start_mod(2)
            split_units(4, 6)
            start_mod(3)
            split_units(6, 16)

            def forget(h):
                ve.wait_ge(sig_done, 3 * h + 1)
                ve.tensor_scalar(f_dec[:, :], gate[:, :], high[:, bass.ds(h, 1)], low[:, bass.ds(h, 1)],
                                 ALU.mult, ALU.add).then_inc(sig_used, 1)

            def chunks(ap):
                return ap[:, :].rearrange("p (c t) -> p c t", t=P)

            def halves(n):
                return pair(n + 1).rearrange("p (c g t) -> p c g t", g=2, t=P // 2)

            def mask_diagonal(n):
                some = slice(n - 1, P, 2)
                ve.copy_predicated(chunks(scores)[:, :, some],
                                   ident[:, some].bitcast(I32).unsqueeze(1).broadcast_to((P, NT, P // 2)),
                                   halves(n)[:, :, 0, :]).then_inc(masked, 1)

            def mask(n, bank_n):
                half = 1 << (n - 1)
                if n > MASKED:
                    for b in range(P // (2 * half)):
                        left = 2 * b * half
                        last = ve.tensor_copy(
                            chunks(scores)[left:left + half, :, left + half:left + 2 * half],
                            ps[left:left + half, bank_n, :].rearrange(
                                "p (c t) -> p c t", t=P // 2)[:, :, b * half:(b + 1) * half])
                    last.then_inc(masked, 1)
                    return
                ve.copy_predicated(
                    scores[:, :].rearrange("p (n two w) -> p n two w", two=2, w=half)[:, :, 1, :],
                    level_mask[:, n - 1, :].bitcast(I32).unsqueeze(1).broadcast_to((P, NT, P // 2)),
                    ps[:, bank_n, :].rearrange("p (n w) -> p n w", w=half) if n > 2 else
                    halves(n)[:, :, 1, :]).then_inc(masked, 1)

            TOTAL_AT = [None, 0] + [T - (T >> (j - 1)) for j in range(2, LEVELS + 1)]

            def total(j):
                n = T >> j
                return f_dec[:, :] if j == 0 else totals[:, TOTAL_AT[j]:TOTAL_AT[j] + n]

            def next_total(j):
                tj = total(j).rearrange("p (n two) -> p n two", two=2)
                ve.tensor_tensor(total(j + 1).unsqueeze(2), tj[:, :, 0:1], tj[:, :, 1:2], ALU.mult)

            def take_level(h, n):
                j = n - 1
                half = 1 << j
                tj = total(j).rearrange("p (n two) -> p n two", two=2)
                blocks = T // (2 * half)
                right = q_dec[:, :].rearrange("p (n two w) -> p n two w", two=2, w=half)[:, :, 1, :]
                left = k_dec[:, :].rearrange("p (n two w) -> p n two w", two=2, w=half)[:, :, 0, :]
                ve.wait_ge(decayed, 8 * h + n)
                ve.wait_ge(scored, LEVELS * h + n)
                if n > 1:
                    ve.wait_ge(masked, TAKES * h + masks(n - 1))
                if n == 1:
                    fours = q_act.rearrange("p (n four) -> p n four", four=4)
                    ve.tensor_copy(fours[:, :, 2:3], fours[:, :, 3:4])
                if n > 2:
                    next_total(j)
                ve.tensor_tensor(right, right, tj[:, :, 0:1].broadcast_to((P, blocks, half)), ALU.mult)
                ve.tensor_tensor(left, left, tj[:, :, 1:2].broadcast_to((P, blocks, half)),
                                 ALU.mult).then_inc(decayed, 1)
                if n <= 2:
                    mask_diagonal(n)
                    ve.wait_ge(masked, TAKES * h + masks(n) - 1)
                    next_total(j)
                mask(n, level_bank[n])

            level_bank = [None, None, None, 4, 5, 4, 5, 4]

            def head_start(h):
                ve.wait_ge(sig_used, 3 * h + 1)
                ve.tensor_scalar(k_dec[:, :], f_dec[:, :], -1.0, 1.0, ALU.mult, ALU.add)
                ve.wait_ge(sig_done, 3 * h + 2)
                ve.tensor_tensor(q_act[:, :], pair(1), gate[:, :], ALU.mult).then_inc(sig_used, 1)
                ve.wait_ge(sig_used, 3 * h + 2)
                ve.tensor_tensor(q_dec[:, :], q_act[:, :], f_dec[:, :], ALU.mult).then_inc(decayed, 1)
                split_w(4 * h + 3, 1)
                for n in (1, 2):
                    take_level(h, n)

            def gate_out(h):
                ve.wait_ge(sig_done, 3 * h + 3)
                ve.tensor_tensor(g_act[:, :], pair(1), gate[:, :], ALU.mult).then_inc(sig_used, 1)

            def head_states(h):
                tot = total(LEVELS)
                kv = pair(2).rearrange("p (c d) -> p c d", d=P)
                ve.wait_ge(chunk_kv, h + 1)
                link(ve.tensor_copy(states[:, 0, :], kv[:, 0, :]))
                for ch in range(1, NT - 1):
                    ins = ve.scalar_tensor_tensor(out=states[:, ch, :], in0=states[:, ch - 1, :],
                                                  scalar=tot[:, ch:ch + 1], in1=kv[:, ch, :],
                                                  op0=ALU.mult, op1=ALU.add)
                    if ch < NT - 2:
                        link(ins)
                ins.then_inc(states_ready, 1)

            def head_norm(h, meanwhile=()):
                o = pair(3).rearrange("p (c d) -> p c d", d=P)
                ve.wait_ge(o_squared, h + 1)
                link(ve.reduce_sum(tiny[:, 2, :], tok[:, :, :], axis=AX_X))
                ve.tensor_scalar(tiny[:, 1, :], tiny[:, 2, :], 1.0 / P, EPS, ALU.mult, ALU.add).then_inc(o_mean, 1)
                for step in meanwhile:
                    step()
                ve.wait_ge(rooted, h + 3)
                ve.tensor_tensor(tok[:, :, :], o, stat[:, 1, :].unsqueeze(2).broadcast_to((P, NT, P)),
                                 ALU.mult).then_inc(o_normed, 1)

            def head_end(h):
                ve.wait_ge(o_turned, h + 1)
                ve.wait_ge(sig_used, 3 * h + 3)
                ve.scalar_tensor_tensor(out=oT[:, h, :], in0=pair(2), scalar=vec_cols[:, 7 * KD:VR],
                                        in1=g_act[:, :], op0=ALU.mult, op1=ALU.mult).then_inc(head_out, 1)

            forget(0)
            split_w(2, 0)
            base, per = own.now, (NT - 2) + 1 + 2 * (JH - 1)
            with ve.Fori(0, H - 1) as h:
                own.restart(base + h * per)
                head_start(h)
                split_w(4 * h + 4, 0)
                for n in range(3, LEVELS + 1):
                    take_level(h, n)
                    if n < LEVELS:
                        ada_quarter(h, n - 3)
                gate_out(h)
                split_w(4 * h + 5, 1)
                head_states(h)
                forget(h + 1)
                head_norm(h)
                split_w(4 * h + 6, 0)
                head_end(h)
                assert own.n == per
            own.restart(base + (H - 1) * per)
            last = H - 1

            def split_wo(k):
                ve.wait_ge(wo_hi, k + 1)
                ve.tensor_tensor(wo_split(k, 1), slabs[:, 1 + k % 2, :], wo_split(k, 0).bitcast(F32),
                                 ALU.subtract).then_inc(wo_lo, 1)

            def split_o(i, q):
                ve.wait_ge(o_hi[q], i + 1)
                ve.tensor_tensor(o_split[:, q, 1, :, :],
                                 oT[:, q * (KD // 2):(q + 1) * (KD // 2), bass.ts(i, P)],
                                 o_split[:, q, 0, :, :].bitcast(F32), ALU.subtract).then_inc(o_lo[q], 1)

            for c in range(3):
                ada_quarter(last, c)
            head_start(last)
            ada_quarter(last, 3)
            for n in range(3, LEVELS + 1):
                take_level(last, n)
                if n == 4:
                    split_wo(0)
                if n == 5:
                    ve.wait_ge(post_in, 16)
                    ve.tensor_tensor(mod_rows[:, 0, :], mod_rows[:, 0, :], slabs[:, 0, :],
                                     ALU.mult).then_inc(mods_made, 1)
                if n == 6:
                    split_wo(1)
            gate_out(last)
            split_wo(2)
            ve.wait_ge(mod_turned, 1)
            modulation(ffn_shift, ffn_scale, vec_cols[:, 2 * KD:3 * KD]).then_inc(mods_made, 1)
            split_o(0, 0)
            head_states(last)
            split_wo(3)
            split_wo(4)
            head_norm(last, (lambda: split_wo(5), lambda: split_o(1, 0)))
            head_end(last)
            split_o(0, 1)
            split_wo(6)
            split_wo(7)
            ve.wait_ge(post_in, 32)
            ve.wait_ge(ada_rowed, PIECES)
            ve.tensor_tensor(mod_rows[:, 3, :], mod_rows[:, 3, :], slabs[:, 0, :], ALU.mult).then_inc(mods_made, 1)

            def make_x1(i, u, times):
                x1 = mod_rows[:, 1 + u, :]
                ve.wait_ge(y_squared, i + 1)
                ve.tensor_scalar(tiny[:, 2, 0:1], tiny[:, 6, 0:1], 1.0 / D, EPS,
                                 ALU.mult, ALU.add).then_inc(y_mean, 1)
                if not isinstance(times, int) or times > 0:
                    ve.wait_ge(x1_stored[u], 16 * times)
                ve.wait_ge(rooted, 2 + H + 2 * i + 1)
                link(ve.scalar_tensor_tensor(out=x1, in0=pair(u), scalar=stat[:, 2, 0:1], in1=mod_rows[:, 0, :],
                                             op0=ALU.mult, op1=ALU.mult))
                ve.wait_ge(xt_in[u], 16 * (times + 1))
                ve.tensor_tensor(x1, x1, slabs[:, 1 + u, :], ALU.add).then_inc(x1_made, 1)

            def mean_x1(i):
                ve.wait_ge(x1_squared, i + 1)
                ve.tensor_scalar(tiny[:, 3, 0:1], tiny[:, 7, 0:1], 1.0 / D, EPS,
                                 ALU.mult, ALU.add).then_inc(x1_mean, 1)

            def split_h2(i, ks=slice(0, KD), scaled=1):
                h2 = norm_tile.rearrange("p (k t) -> p k t", t=P)[:, ks]
                hi, lo = hT[:, 0, ks, bass.ts(i, P)], hT[:, 1, ks, bass.ts(i, P)]
                ve.wait_ge(h2_scaled, i + scaled)
                link(ve.tensor_copy(hi, h2))
                ve.tensor_tensor(lo, h2, hi.bitcast(F32), ALU.subtract).then_inc(h2_split, 1)

            split_o(1, 1)
            make_x1(0, 0, 0)
            mean_x1(0)

            def mixer_tile(i, u, times):
                split_o(i + 1, 0)
                make_x1(i, u, times)
                split_o(i + 1, 1)
                split_h2(i - 1)
                mean_x1(i)

            mixer_tile(1, 1, 0)
            base, per = own.now, 4
            with ve.Fori(1, NT // 2 - 1) as ii:
                own.restart(base + (ii - 1) * per)
                for u in range(2):
                    mixer_tile(2 * ii + u, u, ii)
                assert own.n == per
            own.restart(base + (NT // 2 - 2) * per)
            mixer_tile(NT - 2, 0, NT // 2 - 1)

            def split_up(j, s):
                ve.wait_ge(up_hi[s], j + 1)
                ve.tensor_tensor(up_split[:, s, 1, :, :], up_raw[:, s, :, :],
                                 up_split[:, s, 0, :, :].bitcast(F32), ALU.subtract).then_inc(up_lo[s], 1)

            split_up(0, 0)
            split_up(0, 1)
            make_x1(NT - 1, 1, NT // 2 - 1)
            split_h2(NT - 2)
            mean_x1(NT - 1)
            split_h2(NT - 1, slice(0, KD // 2))
            split_h2(NT - 1, slice(KD // 2, KD), 2)

            def more_taps(j, s, dst):
                ft = j + s * FT
                ve.wait_ge(tap0[s], j + 1)
                link(ve.scalar_tensor_tensor(out=dst[:, 1:T], in0=pair(s)[:, 0:T - 1],
                                             scalar=dw_cols[:, 1, bass.ds(ft, 1)], in1=dst[:, 1:T],
                                             op0=ALU.mult, op1=ALU.add))
                ve.scalar_tensor_tensor(out=dst[:, 2:T], in0=pair(s)[:, 0:T - 2],
                                        scalar=dw_cols[:, 0, bass.ds(ft, 1)], in1=dst[:, 2:T],
                                        op0=ALU.mult, op1=ALU.add).then_inc(conved[s], 1)

            def gate_ffn(j):
                ve.wait_ge(conved[1], j + 1)
                link(ve.tensor_tensor(conv_b, conv_b, conv_a, ALU.mult))
                ve.wait_ge(a_sig, j + 1)
                ve.tensor_tensor(act[:, j, :], conv_b, sig_a, ALU.mult).then_inc(gated, 1)

            base, per = own.now, 3
            with ve.Fori(0, FT - 1) as j:
                own.restart(base + j * per)
                more_taps(j, 0, conv_a)
                split_up(j + 1, 0)
                more_taps(j, 1, conv_b)
                split_up(j + 1, 1)
                gate_ffn(j)
                assert own.n == per
            own.restart(base + (FT - 1) * per)
            more_taps(FT - 1, 0, conv_a)

            def split_down(kk, k, r, s=None):
                s = r % 2 if s is None else s
                ve.wait_ge(a_hi, kk + 1)
                ve.tensor_tensor(a_split[s][:, 1, :], act[:, k, :], a_split[s][:, 0, :].bitcast(F32),
                                 ALU.subtract).then_inc(a_lo, 1)
                ve.wait_ge(wd_hi, kk + 1)
                ve.tensor_tensor(wd_split[s][:, 1, :], wd_raw[r], wd_split[s][:, 0, :].bitcast(F32),
                                 ALU.subtract).then_inc(wd_lo, 1)

            split_down(0, 0, 0)
            more_taps(FT - 1, 1, conv_b)
            split_down(1, 1, 1)
            gate_ffn(FT - 1)
            split_down(2, 2, 2)
            split_down(3, 3, 3)
            with ve.Fori(1, FT // 4) as m:
                for r in range(4):
                    split_down(4 * m + r, 4 * m + r, r)
            split_down(FT - 2, FT - 2, 0)
            split_down(FT - 1, FT - 1, 1)
            split_down(FT, 0, 2)
            g2 = mod_rows[:, 3, :]
            for t in range(NT):
                ve.wait_ge(out_squared, t + 1)
                ve.tensor_tensor(y_gained[:, t, 0:BANK], ps[:, t, :], g2[:, 0:BANK], ALU.mult).then_inc(left_kept, 1)
            split_down(FT + 1, 1, 3)
            ve.tensor_scalar(tiny[:, 5, :], tiny[:, 0, :], 1.0 / D, EPS, ALU.mult, ALU.add).then_inc(left_mean, 1)
            with ve.Fori(0, FT // 4 - 1) as m:
                for r in range(4):
                    split_down(FT + 2 + 4 * m + r, 4 * m + r + 2, r)
            for r in range(3):
                split_down(2 * FT - 4 + r, FT - 4 + r, r)
            split_down(2 * FT - 1, FT - 1, 3, 2)

            def finish(t):
                ve.wait_ge(right_kept, t + 1)
                ve.wait_ge(out_rooted, t + 1)
                ve.wait_ge(x1_back[t], 16)
                ve.scalar_tensor_tensor(out=out_sb[:, t, :], in0=y_gained[:, t, :], scalar=stat[:, 4, t:t + 1],
                                        in1=out_sb[:, t, :], op0=ALU.mult, op1=ALU.add).then_inc(out_made, 1)

            ve.wait_ge(left_mean, 1)
            for t in range(NT):
                ve.wait_ge(out_squared, NT + t + 1)
                ve.tensor_tensor(y_gained[:, t, BANK:D], ps[:, t, :], g2[:, BANK:D], ALU.mult).then_inc(right_kept, 1)
                ve.scalar_tensor_tensor(out=tiny[:, 4, t:t + 1], in0=tiny[:, 1, t:t + 1], scalar=1.0 / D,
                                        in1=tiny[:, 5, t:t + 1], op0=ALU.mult, op1=ALU.add).then_inc(out_mean, 1)
                if t > 0 and t - 1 not in POOL_TILES:
                    finish(t - 1)
            finish(NT - 1)

        @block.tensor
        def _(pe):
            HI, LO = 0, 1
            PARTS = ((HI, HI), (HI, LO), (LO, HI))

            def turn(dst, src, n=P):
                return pe.transpose(dst, src, ident[0:n, 0:n])

            pe.wait_ge(consts_made, 3 + MASKED + 1)
            pe.wait_ge(vec_in, 16 * 6)
            turn(ps[:, 4, 0:VR], vec_rows, VR).then_inc(vecs_turned, 1)
            pe.wait_ge(dw_in, 32)
            for t in range(4):
                last = turn(ps[:, 5, 2 * FT * t:2 * FT * (t + 1)], dw_rows[:, t, :], 2 * FT)
            last.then_inc(dw_turned, 1)

            def spread(p):
                pe.wait_ge(ada_summed, p + 1)
                pe.matmul(ps[:, 6, :], ones[:, :], ada_acc[:, :], start=True, stop=True).then_inc(ada_spread, 1)

            def turn_mods(row):
                for v in range(2):
                    for k in range(KD):
                        last = turn(ps[:, 1, v * KD + k:v * KD + k + 1],
                                    mod_rows[0:1, row + v, k * P:(k + 1) * P], 1)
                last.then_inc(mod_turned, 1)

            def project_tile(s, half, k):
                for n, (a, b) in enumerate(PARTS):
                    last = pe.matmul(ps[:, 2 * s + half, :], w_split[:, s, a, k, :],
                                     hT[:, b, k, half * BANK:(half + 1) * BANK],
                                     start=(k == 0 and n == 0), stop=(k == KD - 1 and n == 2))
                return last

            def project_quarter(s, half, kh, done=None):
                for k in range(kh * (KD // 2), (kh + 1) * (KD // 2)):
                    last = project_tile(s, half, k)
                if done is not None:
                    last.then_inc(done, 1)

            def group(s, quarter, n, freed=None, count=None):
                if quarter == 0:
                    pe.wait_ge(w_lo, n + 1)
                    if freed is not None:
                        pe.wait_ge(freed, count)
                project_quarter(s, quarter // 2, quarter % 2, projected if quarter == 3 else None)

            def chunk(ap, ch):
                return ap[:, ch * P:(ch + 1) * P]

            def level(h, n, bank_n, masked_n=None):
                half = 1 << (n - 1)
                pe.wait_ge(decayed, 8 * h + n)
                if masked_n is not None:
                    pe.wait_ge(masked, TAKES * h + masks(masked_n))
                for ch in range(NT):
                    if n <= 2:
                        fours = q_rows[:, :, n - 1 + ch * P:n - 1 + (ch + 1) * P].rearrange(
                            "p g (n w) -> p g n w", w=2 * n)
                        last = pe.matmul(chunk(pair(n + 1), ch), chunk(k_dec, ch), fours[:, :, :, 0:n],
                                         start=True, stop=True)
                        continue
                    if n <= MASKED:
                        moving = chunk(q_dec, ch).rearrange("p (n two w) -> p n two w", two=2, w=half)[:, :, 1, :]
                        last = pe.matmul(ps[:, bank_n, ch * (P // 2):(ch + 1) * (P // 2)], chunk(k_dec, ch), moving,
                                         start=True, stop=True)
                        continue
                    for b in range(P // (2 * half)):
                        left, at = 2 * b * half, ch * (P // 2) + b * half
                        last = pe.matmul(ps[left:left + half, bank_n, at:at + half],
                                         chunk(k_dec, ch)[:, left:left + half],
                                         chunk(q_dec, ch)[:, left + half:left + 2 * half], start=True, stop=True)
                last.then_inc(scored, 1)

            def turn_values(h):
                pe.wait_ge(values_copied, h + 1)
                pe.wait_ge(masked, TAKES * h + masks(2))
                for ch in range(NT):
                    last = turn(chunk(pair(3), ch), chunk(gate, ch))
                last.then_inc(values_turned, 1)

            def turn_keys(h):
                pe.wait_ge(decayed, 8 * h + 8)
                pe.wait_ge(v_ready, h + 1)
                for ch in range(NT):
                    last = turn(chunk(pair(3), ch), chunk(k_dec, ch))
                last.then_inc(keys_turned, 1)

            def keys_values(h):
                pe.wait_ge(keys_ready, h + 1)
                pe.wait_ge(masked, TAKES * h + TAKES)
                for ch in range(NT - 1):
                    last = pe.matmul(chunk(pair(2), ch), tok[:, ch, :], v_tok[:, ch, :], start=True, stop=True)
                last.then_inc(chunk_kv, 1)

            def outputs(h):
                pe.wait_ge(ada_rowed, h + 1)
                pe.wait_ge(states_ready, h + 1)
                for ch in range(NT):
                    last = pe.matmul(chunk(pair(3), ch), chunk(scores, ch), v_tok[:, ch, :],
                                     start=True, stop=(ch == 0))
                    if ch > 0:
                        last = pe.matmul(chunk(pair(3), ch), chunk(q_dec, ch), states[:, ch - 1, :],
                                         start=False, stop=True)
                last.then_inc(o_ready, 1)

            def turn_outputs(h):
                pe.wait_ge(o_normed, h + 1)
                for ch in range(NT):
                    last = turn(chunk(pair(2), ch), tok[:, ch, :])
                last.then_inc(o_turned, 1)

            def turn_unit(u):
                k, half = UNITS[u]
                pe.wait_ge(x_normed, (half + 1) * (NT // 2))
                if UNIT_BEFORE[u] is not None:
                    pe.wait_ge(h_scaled, UNIT_BEFORE[u] + 1)
                for n in range(NT // 2):
                    last = turn(ps[:, UNIT_BANK[u], n * P:(n + 1) * P],
                                x_sb[:, half * (NT // 2) + n, k * P:(k + 1) * P])
                last.then_inc(x_turned, 1)

            def start_piece(p):
                m = 2 * p + 1
                row = ps[0:1, ROW_BANK[p], :]
                pe.wait_ge(start_in[m], 16)
                if p > 0 and ROW_BANK[p] == ROW_BANK[p - 1]:
                    pe.wait_ge(mix_made, p)
                for k in range(KD - START_PE, KD):
                    pe.matmul(row, cond[:, k:k + 1], ada_slot[m % len(ada_slot)][:, k - JH, :],
                              start=(k == KD - START_PE), stop=False)
                pe.wait_ge(start_summed, p + 1)
                pe.matmul(row, ones[:, 0:1], start_acc[p % 2], start=False, stop=True).then_inc(start_rowed, 1)

            def turn_start(p):
                pe.wait_ge(start_copied, p + 1)
                for tile in range(CP):
                    last = turn(ps[:, ROW_BANK[p], tile:tile + 1], start_row[:, tile * P:(tile + 1) * P], 1)
                last.then_inc(start_turned, 1)

            def start_products(s, half, ks):
                pe.wait_ge(w_lo, s + 1)
                for k in ks:
                    if s == 0:
                        pe.wait_ge(h_split, UNITS.index((k, half)) + 1)
                    last = project_tile(s, half, k)
                if (half, k) == (1, KD - 1):
                    last.then_inc(projected, 1)

            def keep_warm(n):
                for _ in range(n):
                    pe.matmul(ps[:, 1, :], ones[:, :], x_sb[:, 0, 0:BANK], start=True, stop=True)

            first, second = range(KD // 2), range(KD // 2, KD)
            pe.wait_ge(vecs_copied, 2)
            for u in range(4):
                turn_unit(u)
            pe.wait_ge(x_squared, NT)
            keep_warm(1)
            turn_unit(4)
            pe.wait_ge(cond_made, 1)
            start_piece(0)
            turn_start(0)
            keep_warm(2)
            start_piece(1)
            keep_warm(1)
            turn_start(1)
            keep_warm(2)
            for u in (5, 6, 7):
                turn_unit(u)
                keep_warm(1)
            start_piece(2)
            start_products(0, 0, first)
            turn_start(2)
            for u in (8, 9, 10):
                turn_unit(u)
            start_piece(3)
            start_products(1, 0, first[:1])
            turn_start(3)
            start_products(1, 0, first[1:])
            turn_unit(11)
            start_products(0, 1, first)
            pe.wait_ge(mix_made, START_PIECES)
            start_products(1, 1, first[:2])
            turn_unit(12)
            start_products(1, 1, first[2:])
            turn_unit(13)
            start_products(0, 0, second[:1])
            turn_unit(14)
            start_products(0, 0, second[1:2])
            turn_unit(15)
            start_products(0, 0, second[2:])
            start_products(0, 1, second)
            start_products(1, 0, second)
            start_products(1, 1, second)

            def head_first_half(h):
                for quarter in range(4):
                    group(0, quarter, 4 * h + 2, sig_done, 3 * h + 1)
                    if quarter == 1:
                        level(h, 1, None)
                    if quarter == 2:
                        level(h, 2, None)
                    if quarter == 3:
                        level(h, 3, 4, 1)
                for quarter in range(4):
                    group(1, quarter, 4 * h + 3, sig_used, 3 * h + 2)
                    if quarter == 0:
                        turn_values(h)
                        level(h, 4, 5)
                    if quarter == 1:
                        level(h, 5, 4, 3)
                    if quarter == 2:
                        level(h, 6, 5, 4)
                    if quarter == 3:
                        level(h, 7, 4, 5)

            with pe.Fori(0, H - 1) as h:
                head_first_half(h)
                for quarter in range(4):
                    group(0, quarter, 4 * h + 4, values_copied, h + 1)
                    if quarter == 0:
                        turn_keys(h)
                    if quarter == 1:
                        keys_values(h)
                    if quarter == 2:
                        spread(h)
                    if quarter == 3:
                        outputs(h)
                for quarter in range(4):
                    group(1, quarter, 4 * h + 5, sig_used, 3 * h + 3)
                    if quarter == 2:
                        turn_outputs(h)
            def mix_out(i, u, q, kqs=range(KD // 2), first=False):
                pe.wait_ge(o_lo[q], i + 1)
                for kq in kqs:
                    k = q * (KD // 2) + kq
                    if first:
                        pe.wait_ge(wo_lo, k + 1)
                    for half in range(2):
                        for n, (a, b) in enumerate(PARTS):
                            last = pe.matmul(ps[:, 2 * u + half, :], o_split[:, q, a, kq, :],
                                             wo_split(k, b)[:, half * BANK:(half + 1) * BANK],
                                             start=(k == 0 and n == 0), stop=(k == KD - 1 and n == 2))
                if kqs[-1] == KD // 2 - 1:
                    last.then_inc(o_used[q], 1)

            last_head = H - 1
            head_first_half(last_head)
            pe.wait_ge(v_ready, H)
            spread(PIECES - 1)
            pe.wait_ge(ada_rowed, PIECES)
            turn_keys(last_head)
            turn_mods(1)
            keys_values(last_head)
            pe.wait_ge(mods_made, 2)
            mix_out(0, 0, 0, range(0, 2), True)
            outputs(last_head)
            mix_out(0, 0, 0, range(2, 4), True)
            pe.wait_ge(sig_used, 3 * H)
            mix_out(1, 1, 0, range(0, 1))
            turn_outputs(last_head)
            mix_out(1, 1, 0, range(1, 3))
            mix_out(0, 0, 1, first=True)
            mix_out(1, 1, 0, range(3, 4))
            mix_out(1, 1, 1)

            def turn_x1(i):
                pe.wait_ge(x1_normed, i + 1)
                for k in range(KD):
                    last = turn(chunk(pair(2), k), chunk(norm_tile, k))
                last.then_inc(x1_turned, 1)

            turn_x1(0)
            with pe.Fori(0, NT // 2 - 1) as ii:
                for u in range(2):
                    i = 2 * ii + 2 + u
                    pe.wait_ge(x1_made, 2 * ii + u + 1)
                    for q in range(2):
                        mix_out(i, u, q)
                    turn_x1(i - 1)

            def up_half(s, half, done=None, ks=range(KD)):
                for k in ks:
                    for n, (a, b) in enumerate(PARTS):
                        last = pe.matmul(ps[:, 2 * s + half, :], up_split[:, s, a, k, :],
                                         hT[:, b, k, half * BANK:(half + 1) * BANK],
                                         start=(k == 0 and n == 0), stop=(k == KD - 1 and n == 2))
                if done is not None:
                    last.then_inc(done, 1)

            pe.wait_ge(x1_made, NT - 1)
            pe.wait_ge(up_lo[0], 1)
            pe.wait_ge(h2_split, NT // 2)
            up_half(0, 0)
            pe.wait_ge(x1_made, NT)
            pe.wait_ge(up_lo[1], 1)
            up_half(1, 0, ks=range(0, KD // 2))
            turn_x1(NT - 1)
            up_half(1, 0, ks=range(KD // 2, KD))
            pe.wait_ge(h2_split, NT)
            up_half(0, 1, ks=range(0, KD // 2))
            pe.wait_ge(h2_split, NT + 1)
            up_half(0, 1, upped[0], range(KD // 2, KD))
            up_half(1, 1, upped[1])
            with pe.Fori(1, FT) as j:
                for s in range(2):
                    pe.wait_ge(up_lo[s], j + 1)
                    pe.wait_ge(conved[s], j)
                    up_half(s, 0)
                    up_half(s, 1, upped[s])

            def down_tile(s, t, start, stop):
                for n, (a, b) in enumerate(PARTS):
                    last = pe.matmul(ps[:, t, :], a_split[s][:, a, t * P:(t + 1) * P], wd_split[s][:, b, :],
                                     start=(start and n == 0), stop=(stop and n == 2))
                return last

            def down_step(kk, s):
                pe.wait_ge(wd_lo, kk + 1)
                for t in range(NT):
                    last = down_tile(s, t, False, False)
                last.then_inc(downed, 1)

            def down_half(half):
                base = half * FT
                pe.wait_ge(wd_lo, base + 1)
                for t in (4, 5, 6, 7, 0, 1, 2, 3) if half == 0 else range(NT):
                    if half == 1:
                        pe.wait_ge(left_kept, t + 1)
                    elif t in (0, 2):
                        pe.wait_ge(conved[t // 2], FT)
                    last = down_tile(0, t, True, False)
                last.then_inc(downed, 1)
                down_step(base + 1, 1)
                with pe.Fori(1, FT // 2 - 2) as kk:
                    for s in range(2):
                        down_step(base + 2 * kk + s, s)
                down_step(base + FT - 4, 0)
                if half == 0:
                    down_step(base + FT - 3, 1)
                    down_step(base + FT - 2, 0)
                    pe.wait_ge(wd_lo, base + FT)
                    for t in range(NT):
                        down_tile(1, t, False, True).then_inc(y_bank, 1)
                    return
                ready = {1: FT - 2, 0: FT - 1, 2: FT}
                for s, t in ([(1, t) for t in range(5)] + [(0, t) for t in range(3)] + [(2, t) for t in range(3)] +
                             [(0, 3), (2, 3), (0, 4), (2, 4)] + [(s, t) for t in range(5, NT) for s in (1, 0, 2)]):
                    if s in ready:
                        pe.wait_ge(wd_lo, base + ready.pop(s))
                    last = down_tile(s, t, False, s == 2)
                    if s == 2:
                        last.then_inc(y_bank, 1)

            down_half(0)
            down_half(1)


_INS = ["x", "c", "ada_w", "ada_b", "pre_mix_g", "post_mix_g", "pre_ffn_g", "post_ffn_g", "hgrn_w_in",
        "hgrn_lb_logits", "hgrn_gnorm_g", "hgrn_w_out", "ffn_w_up", "ffn_dw_w", "ffn_dw_b", "ffn_w_down"]


def kernel(**inputs):
    import numpy as _np
    import concourse.bacc as _bacc
    from concourse import mybir as _mybir
    from concourse.bass_utils import run_bass_kernel_spmd as _run

    nc = _bacc.Bacc("TRN2", target_bir_lowering=False, num_devices=1)
    arrays, args = {}, []
    for name in _INS:
        a = _np.ascontiguousarray(inputs[name])
        arrays[f"in_{name}"] = a
        args.append(nc.dram_tensor(f"in_{name}", a.shape, _mybir.dt.from_np(a.dtype), kind="ExternalInput").ap())
    shape = arrays["in_x"].shape
    args.append(nc.dram_tensor("out_x", shape, _mybir.dt.from_np(_np.dtype("float32")), kind="ExternalOutput").ap())
    hybrid_layer(nc, *args)
    r = _run(nc, [arrays], core_ids=[0])
    return r.results[0]["out_x"]
```
